# Optimizing a Trainium2 kernel written in Bass

```python
import jax
import jax.numpy as jnp
from jax import lax
import numpy as np

D_MODEL = 1024
BATCH = 1
SEQ = 1024
DEPTH = 2

N_MIXERS = 2
GRID_W = 64
N_MEM = 256
MEM_HEADS = 4
MEM_DH = 64
MEM_W = MEM_HEADS * MEM_DH
NA_HEADS = 12
NA_DH = 64
NA_W = NA_HEADS * NA_DH
WIN_H_MAX = 8
WIN_W = 16
ML_HEADS = 4
ML_DH = 192
ML_W = ML_HEADS * ML_DH
CONV_K = 5
CHUNK = 128
MIX_W = NA_W + MEM_W
N_EXPERTS = 16
N_GROUPS = 4
EXPERTS_PER_GROUP = N_EXPERTS // N_GROUPS
TOP_K = 2
D_EXPERT = 512
MOE_BLOCK = 128
ALPHA = (2 * DEPTH) ** 0.25
BETA = (8 * DEPTH) ** -0.25
LN_EPS = 1e-5


def layer_norm(x, g, b):
    xf = x.astype(jnp.float32)
    mu = jnp.mean(xf, axis=-1, keepdims=True)
    var = jnp.mean(jnp.square(xf - mu), axis=-1, keepdims=True)
    return ((xf - mu) * lax.rsqrt(var + LN_EPS) * g + b).astype(x.dtype)

def memory_attention(q, mem_k, mem_v):
    B, S, _ = q.shape
    q = q.reshape(B, S, MEM_HEADS, MEM_DH) * (MEM_DH ** -0.5)
    s = jnp.einsum('bshd,bmhd->bhsm', q, mem_k, preferred_element_type=jnp.float32)
    p = jax.nn.softmax(s, axis=-1).astype(mem_v.dtype)
    return jnp.einsum('bhsm,bmhd->bshd', p, mem_v).reshape(B, S, MEM_W)

def neighbourhood_attention(q, k, v, rpb):
    B, R, W, H, Dh = q.shape
    win_h = min(WIN_H_MAX, R)
    n_cb = W // WIN_W
    span = 2 * WIN_W
    q_cols = np.arange(W).reshape(n_cb, WIN_W)
    cb_start = np.clip(np.arange(n_cb) * WIN_W - WIN_W // 2, 0, W - span)
    key_cols = cb_start[:, None] + np.arange(span)[None, :]
    col_start = np.clip(q_cols - WIN_W // 2, 0, W - WIN_W)
    kc = key_cols[:, None, :]
    col_in = (kc >= col_start[..., None]) & (kc < col_start[..., None] + WIN_W)
    dc_idx = np.clip(kc - q_cols[..., None] + WIN_W - 1, 0, 2 * WIN_W - 2)
    rpb_c = jnp.transpose(rpb[:, :, dc_idx], (0, 2, 3, 1, 4))

    def row_block(r):
        rs = jnp.clip(r - win_h // 2, 0, R - win_h)
        k_rows = lax.dynamic_slice_in_dim(k, rs, win_h, axis=1)
        v_rows = lax.dynamic_slice_in_dim(v, rs, win_h, axis=1)
        k_blk = k_rows[:, :, key_cols]
        v_blk = v_rows[:, :, key_cols]
        q_blk = lax.dynamic_index_in_dim(q, r, axis=1, keepdims=False).reshape(B, n_cb, WIN_W, H, Dh)
        s = jnp.einsum('bjqhd,brjkhd->bhjqrk', q_blk, k_blk, preferred_element_type=jnp.float32)
        dr = rs + jnp.arange(win_h) - r + WIN_H_MAX - 1
        s = s + jnp.take(rpb_c, dr, axis=3)[None].astype(jnp.float32)
        s = jnp.where(col_in[:, :, None, :], s, -jnp.inf)
        p = jax.nn.softmax(s.reshape(B, H, n_cb, WIN_W, win_h * span), axis=-1)
        p = p.reshape(s.shape).astype(v.dtype)
        o = jnp.einsum('bhjqrk,brjkhd->bjqhd', p, v_blk)
        return o.reshape(B, W, H, Dh)

    out = lax.map(row_block, jnp.arange(R))
    return jnp.moveaxis(out, 0, 1)

def na_mixer(x, w_in, rpb, mem_k, mem_v):
    B, S, _ = x.shape
    rows = S // GRID_W
    h = x @ w_in
    q, k, v, q_mem = jnp.split(h, [NA_W, 2 * NA_W, 3 * NA_W], axis=-1)
    grid = (B, rows, GRID_W, NA_HEADS, NA_DH)
    y = neighbourhood_attention(q.reshape(grid) * (NA_DH ** -0.5), k.reshape(grid), v.reshape(grid), rpb)
    return jnp.concatenate([y.reshape(B, S, NA_W), memory_attention(q_mem, mem_k, mem_v)], axis=-1)

def mlstm_chunkwise(q, k, v, i_pre, f_pre):
    q, k, v = q.astype(jnp.float32), k.astype(jnp.float32), v.astype(jnp.float32)
    B, H, S, Dk = q.shape
    Dv = v.shape[-1]
    nc = S // CHUNK
    log_f = jax.nn.log_sigmoid(f_pre.astype(jnp.float32))
    i_pre = i_pre.astype(jnp.float32)

    def to_chunks(a):
        return jnp.moveaxis(a.reshape(a.shape[:2] + (nc, CHUNK) + a.shape[3:]), 2, 0)

    causal = np.tril(np.ones((CHUNK, CHUNK), dtype=bool))

    def step(carry, inp):
        C, n, m = carry
        qb, kb, vb, ib, fb = inp
        b = jnp.cumsum(fb, axis=-1)
        d = jnp.where(causal, b[..., :, None] - b[..., None, :] + ib[..., None, :], -jnp.inf)
        inter = b + m[..., None]
        m_t = jnp.maximum(jnp.max(d, axis=-1), inter)
        dexp = jnp.exp(d - m_t[..., None])
        iexp = jnp.exp(inter - m_t)
        s = jnp.einsum('bhtd,bhsd->bhts', qb, kb) * dexp
        num = jnp.einsum('bhts,bhse->bhte', s, vb) + iexp[..., None] * jnp.einsum('bhtd,bhde->bhte', qb, C)
        den = jnp.sum(s, axis=-1) + iexp * jnp.einsum('bhtd,bhd->bht', qb, n)
        h = num / jnp.maximum(jnp.abs(den), jnp.exp(-m_t))[..., None]
        b_last = b[..., -1]
        w_s = b_last[..., None] - b + ib
        m_new = jnp.maximum(b_last + m, jnp.max(w_s, axis=-1))
        wexp = jnp.exp(w_s - m_new[..., None])
        cexp = jnp.exp(b_last + m - m_new)
        C_new = cexp[..., None, None] * C + jnp.einsum('bhs,bhsd,bhse->bhde', wexp, kb, vb)
        n_new = cexp[..., None] * n + jnp.einsum('bhs,bhsd->bhd', wexp, kb)
        return (C_new, n_new, m_new), h

    init = (jnp.zeros((B, H, Dk, Dv), jnp.float32), jnp.zeros((B, H, Dk), jnp.float32),
            jnp.zeros((B, H), jnp.float32))
    _, hs = lax.scan(step, init, (to_chunks(q), to_chunks(k), to_chunks(v), to_chunks(i_pre), to_chunks(log_f)))
    return jnp.moveaxis(hs, 0, 2).reshape(B, H, S, Dv)

def mlstm_mixer(x, w_in, conv_w, conv_b, w_qkv, gate_b, norm_g, skip, mem_k, mem_v):
    B, S, _ = x.shape
    h = x @ w_in
    xm, z, gates, q_mem = jnp.split(h, [ML_W, 2 * ML_W, 2 * ML_W + 4 * ML_HEADS], axis=-1)
    xc = lax.conv_general_dilated(xm, conv_w[:, None, :], window_strides=(1,), padding='SAME',
                                  dimension_numbers=('NWC', 'WIO', 'NWC'), feature_group_count=ML_W)
    xc = jax.nn.silu(xc + conv_b)
    xc_h = xc.reshape(B, S, ML_HEADS, ML_DH)
    xm_h = xm.reshape(B, S, ML_HEADS, ML_DH)
    q = jnp.einsum('bshd,hde->bhse', xc_h, w_qkv[0])
    k = jnp.einsum('bshd,hde->bhse', xc_h, w_qkv[1]) * (ML_DH ** -0.5)
    v = jnp.einsum('bshd,hde->bhse', xm_h, w_qkv[2])
    g = (gates.reshape(B, S, 4, ML_HEADS) + gate_b).astype(jnp.float32)
    g = jnp.transpose(g, (2, 0, 3, 1))
    h_f = mlstm_chunkwise(q, k, v, g[0], g[1])
    h_b = jnp.flip(mlstm_chunkwise(jnp.flip(q, 2), jnp.flip(k, 2), jnp.flip(v, 2),
                                   jnp.flip(g[2], -1), jnp.flip(g[3], -1)), 2)
    hs = h_f + h_b
    mu = jnp.mean(hs, axis=-1, keepdims=True)
    var = jnp.mean(jnp.square(hs - mu), axis=-1, keepdims=True)
    hs = (hs - mu) * lax.rsqrt(var + LN_EPS)
    hs = jnp.transpose(hs, (0, 2, 1, 3)).reshape(B, S, ML_W) * norm_g
    y = ((hs + skip * xc) * jax.nn.silu(z)).astype(x.dtype)
    return jnp.concatenate([y, memory_attention(q_mem, mem_k, mem_v)], axis=-1)

def moe(x, router_w, router_b, w_gate, w_up, w_down):
    B, S, D = x.shape
    N = B * S
    xf = x.reshape(N, D)
    scores = jax.nn.sigmoid(jnp.matmul(xf, router_w, preferred_element_type=jnp.float32))
    biased = scores + router_b.astype(jnp.float32)
    grp_score = jnp.sum(lax.top_k(biased.reshape(N, N_GROUPS, EXPERTS_PER_GROUP), 2)[0], axis=-1)
    g_sel = jnp.argmax(grp_score, axis=-1)
    in_group = (jnp.arange(N_EXPERTS) // EXPERTS_PER_GROUP)[None, :] == g_sel[:, None]
    _, idx = lax.top_k(jnp.where(in_group, biased, -jnp.inf), TOP_K)
    w = jnp.take_along_axis(scores, idx, axis=1)
    w = w / jnp.sum(w, axis=-1, keepdims=True)
    NK = N * TOP_K
    flat_e = idx.reshape(NK)
    order = jnp.argsort(flat_e)
    e_sorted = flat_e[order]
    tok_sorted = order // TOP_K
    counts = jnp.bincount(flat_e, length=N_EXPERTS)
    padded = (counts + MOE_BLOCK - 1) // MOE_BLOCK * MOE_BLOCK
    pad_end = jnp.cumsum(padded)
    pad_start = pad_end - padded
    start = jnp.cumsum(counts) - counts
    dest = pad_start[e_sorted] + jnp.arange(NK) - start[e_sorted]
    n_blocks = -(-NK // MOE_BLOCK) + N_EXPERTS
    buf = jnp.zeros((n_blocks * MOE_BLOCK, D), x.dtype).at[dest].set(xf[tok_sorted])
    block_e = jnp.minimum(jnp.searchsorted(pad_end, jnp.arange(n_blocks) * MOE_BLOCK, side='right'),
                          N_EXPERTS - 1)

    def expert_block(args):
        xb, e = args
        hb = jax.nn.silu(xb @ w_gate[e]) * (xb @ w_up[e])
        return hb @ w_down[e]

    y = lax.map(expert_block, (buf.reshape(n_blocks, MOE_BLOCK, D), block_e)).reshape(n_blocks * MOE_BLOCK, D)
    w_sorted = w.reshape(NK)[order].astype(x.dtype)
    out = jnp.zeros((N, D), x.dtype).at[tok_sorted].add(y[dest] * w_sorted[:, None])
    return out.reshape(B, S, D)

def first_inputs(seed: int = 0) -> dict:
    key = jax.random.key(seed)
    ks = jax.random.split(key, 26)
    n_a = (DEPTH + 1) // 2
    n_b = DEPTH // 2

    def nrm(k, shape, scale):
        return jax.random.normal(k, shape, jnp.float32) * scale

    x = nrm(ks[0], (BATCH, SEQ, D_MODEL), 1.0)
    mem = nrm(ks[1], (BATCH, N_MEM, D_MODEL), 1.0)
    mem_ln_g = 1.0 + nrm(ks[2], (D_MODEL,), 0.05)
    mem_ln_b = nrm(ks[3], (D_MODEL,), 0.02)
    w_mem_kv = nrm(ks[4], (D_MODEL, 2 * MEM_W), D_MODEL ** -0.5).at[:, MEM_W:].multiply(BETA)
    router_w = nrm(ks[5], (D_MODEL, N_EXPERTS), D_MODEL ** -0.5)
    router_b = nrm(ks[6], (N_EXPERTS,), 0.01)
    na_w_in = nrm(ks[7], (n_a, D_MODEL, 3 * NA_W + MEM_W), D_MODEL ** -0.5)
    na_w_in = na_w_in.at[:, :, 2 * NA_W:3 * NA_W].multiply(BETA)
    na_rpb = nrm(ks[8], (n_a, NA_HEADS, 2 * WIN_H_MAX - 1, 2 * WIN_W - 1), 0.1)
    ml_w_in = nrm(ks[9], (n_b, D_MODEL, 2 * ML_W + 4 * ML_HEADS + MEM_W), D_MODEL ** -0.5)
    ml_conv_w = nrm(ks[10], (n_b, CONV_K, ML_W), CONV_K ** -0.5)
    ml_conv_b = nrm(ks[11], (n_b, ML_W), 0.02)
    ml_w_qkv = nrm(ks[12], (n_b, 3, ML_HEADS, ML_DH, ML_DH), ML_DH ** -0.5).at[:, 2].multiply(BETA)
    i_bias = nrm(ks[13], (n_b, 2, ML_HEADS), 0.1)
    f_bias = jnp.linspace(3.0, 6.0, ML_HEADS)[None, None, :] + nrm(ks[14], (n_b, 2, ML_HEADS), 0.1)
    ml_gate_b = jnp.stack([i_bias[:, 0], f_bias[:, 0], i_bias[:, 1], f_bias[:, 1]], axis=1)
    ml_norm_g = 1.0 + nrm(ks[15], (n_b, ML_W), 0.05)
    ml_skip = 1.0 + nrm(ks[16], (n_b, ML_W), 0.05)
    w_out = nrm(ks[17], (DEPTH, MIX_W, D_MODEL), MIX_W ** -0.5 * BETA)
    ln_g = 1.0 + nrm(ks[18], (DEPTH, 2, D_MODEL), 0.05)
    ln_b = nrm(ks[19], (DEPTH, 2, D_MODEL), 0.02)
    exp_w_gate = nrm(ks[20], (DEPTH, N_EXPERTS, D_MODEL, D_EXPERT), D_MODEL ** -0.5)
    exp_w_up = nrm(ks[21], (DEPTH, N_EXPERTS, D_MODEL, D_EXPERT), D_MODEL ** -0.5)
    exp_w_down = nrm(ks[22], (DEPTH, N_EXPERTS, D_EXPERT, D_MODEL), D_EXPERT ** -0.5 * BETA)
    return {'x': x, 'mem': mem, 'mem_ln_g': mem_ln_g, 'mem_ln_b': mem_ln_b, 'w_mem_kv': w_mem_kv,
            'router_w': router_w, 'router_b': router_b, 'na_w_in': na_w_in, 'na_rpb': na_rpb,
            'ml_w_in': ml_w_in, 'ml_conv_w': ml_conv_w, 'ml_conv_b': ml_conv_b, 'ml_w_qkv': ml_w_qkv,
            'ml_gate_b': ml_gate_b, 'ml_norm_g': ml_norm_g, 'ml_skip': ml_skip, 'w_out': w_out,
            'ln_g': ln_g, 'ln_b': ln_b, 'exp_w_gate': exp_w_gate, 'exp_w_up': exp_w_up,
            'exp_w_down': exp_w_down}

def first_block(x, mem, mem_ln_g, mem_ln_b, w_mem_kv, router_w, router_b, na_w_in, na_rpb,
              ml_w_in, ml_conv_w, ml_conv_b, ml_w_qkv, ml_gate_b, ml_norm_g, ml_skip, w_out,
              ln_g, ln_b, exp_w_gate, exp_w_up, exp_w_down):
    B, M, _ = mem.shape
    mem_k, mem_v = jnp.split(layer_norm(mem, mem_ln_g, mem_ln_b) @ w_mem_kv, 2, axis=-1)
    mem_k = mem_k.reshape(B, M, MEM_HEADS, MEM_DH)
    mem_v = mem_v.reshape(B, M, MEM_HEADS, MEM_DH)
    for i in range(DEPTH):
        j = i // N_MIXERS
        if i % N_MIXERS == 0:
            mixed = na_mixer(x, na_w_in[j], na_rpb[j], mem_k, mem_v)
        else:
            mixed = mlstm_mixer(x, ml_w_in[j], ml_conv_w[j], ml_conv_b[j], ml_w_qkv[j], ml_gate_b[j],
                                ml_norm_g[j], ml_skip[j], mem_k, mem_v)
        x = layer_norm(ALPHA * x + mixed @ w_out[i], ln_g[i, 0], ln_b[i, 0])
        x = layer_norm(ALPHA * x + moe(x, router_w, router_b, exp_w_gate[i], exp_w_up[i], exp_w_down[i]),
                       ln_g[i, 1], ln_b[i, 1])
    return x


CHUNK_2 = 64
Q_BLOCK = 128
EPS = 1e-6
ROPE_THETA = 10000.0

RET_HEADS = 4
RET_HEAD_DIM = 64
RET_WIDTH = RET_HEADS * RET_HEAD_DIM

MLA_HEADS = 8
MLA_NOPE = 64
MLA_ROPE = 32
MLA_V = 64
MLA_WIDTH = MLA_HEADS * MLA_V
MLA_Q_RANK = 256
MLA_KV_RANK = 128

GLA_HEADS = 4
GLA_DK = 32
GLA_DV = 64
GLA_KWIDTH = GLA_HEADS * GLA_DK
GLA_WIDTH = GLA_HEADS * GLA_DV
GLA_GATE_RANK = 16
GLA_TAU = 16.0

MIX_WIDTH = RET_WIDTH + MLA_WIDTH + GLA_WIDTH

RET_SPLIT = (RET_WIDTH, RET_WIDTH, RET_WIDTH, RET_WIDTH)
MLA_SPLIT = (MLA_Q_RANK, MLA_KV_RANK, MLA_ROPE, MLA_WIDTH)
GLA_SPLIT = (GLA_KWIDTH, GLA_KWIDTH, GLA_WIDTH, GLA_GATE_RANK, GLA_WIDTH)
IN_COLS = sum(RET_SPLIT) + sum(MLA_SPLIT) + sum(GLA_SPLIT)


def rms_norm(x, w=None):
    xf = x.astype(jnp.float32)
    y = xf * lax.rsqrt(jnp.mean(xf * xf, axis=-1, keepdims=True) + EPS)
    if w is not None:
        y = y * w.astype(jnp.float32)
    return y.astype(x.dtype)

def split_cols(t, sizes):
    cuts = [int(s) for s in np.cumsum(sizes)[:-1]]
    return jnp.split(t, cuts, axis=-1)

def to_heads(t, n_heads):
    b, s, _ = t.shape
    return t.reshape(b, s, n_heads, -1)

def rope(x, pos):
    half = x.shape[-1] // 2
    inv = ROPE_THETA ** (-jnp.arange(half, dtype=jnp.float32) / half)
    ang = pos.astype(jnp.float32)[..., None] * inv
    cos = jnp.cos(ang)[:, :, None, :]
    sin = jnp.sin(ang)[:, :, None, :]
    x1 = x[..., :half].astype(jnp.float32)
    x2 = x[..., half:].astype(jnp.float32)
    out = jnp.concatenate([x1 * cos - x2 * sin, x2 * cos + x1 * sin], axis=-1)
    return out.astype(x.dtype)

def chunk_states(u, a):
    u_t = jnp.moveaxis(u, 1, 0)
    a_t = jnp.moveaxis(a, 1, 0)

    def step(s, inp):
        ui, ai = inp
        return ai[..., None] * s + ui, s

    _, s_prev = lax.scan(step, jnp.zeros_like(u_t[0]), (u_t, a_t))
    return jnp.moveaxis(s_prev, 0, 1)

def retention(q, k, v):
    b, s, h, d = q.shape
    dv = v.shape[-1]
    nc = s // CHUNK_2
    f32 = jnp.float32
    log_gamma = jnp.log1p(-jnp.exp2(-5.0 - jnp.arange(h, dtype=f32)))
    q = q.astype(f32).reshape(b, nc, CHUNK_2, h, d)
    k = k.astype(f32).reshape(b, nc, CHUNK_2, h, d) * (d ** -0.5)
    v = v.astype(f32).reshape(b, nc, CHUNK_2, h, dv)
    idx = jnp.arange(CHUNK_2, dtype=f32)
    decay = jnp.exp(log_gamma[:, None, None] * jnp.abs(idx[:, None] - idx[None, :]))
    scores = jnp.einsum('bnihd,bnjhd->bnhij', q, k) * decay
    intra = jnp.einsum('bnhij,bnjhe->bnihe', scores, v)
    k_w = jnp.exp((CHUNK_2 - 1.0 - idx)[:, None] * log_gamma[None, :])
    u = jnp.einsum('bnjhd,jh,bnjhe->bnhde', k, k_w, v)
    a = jnp.broadcast_to(jnp.exp(CHUNK_2 * log_gamma)[:, None], (b, nc, h, d))
    s_prev = chunk_states(u, a)
    q_w = jnp.exp((idx + 1.0)[:, None] * log_gamma[None, :])
    inter = jnp.einsum('bnihd,ih,bnhde->bnihe', q, q_w, s_prev)
    return (intra + inter).reshape(b, s, h, dv)

def mla(q_lat, kv_lat, k_rope, q_norm_w, w_uq, kv_norm_w, w_ukv, pos):
    b, s, _ = q_lat.shape
    q = (rms_norm(q_lat, q_norm_w) @ w_uq).reshape(b, s, MLA_HEADS, MLA_NOPE + MLA_ROPE)
    q_nope = q[..., :MLA_NOPE]
    q_pe = rope(q[..., MLA_NOPE:], pos)
    kv = (rms_norm(kv_lat, kv_norm_w) @ w_ukv).reshape(b, s, MLA_HEADS, MLA_NOPE + MLA_V)
    k_nope = kv[..., :MLA_NOPE]
    v = kv[..., MLA_NOPE:]
    k_pe = rope(k_rope[:, :, None, :], pos)[:, :, 0, :]
    scale = (MLA_NOPE + MLA_ROPE) ** -0.5
    key_chunk = jnp.arange(s) // CHUNK_2
    nb = s // Q_BLOCK
    qn_b = jnp.moveaxis(q_nope.reshape(b, nb, Q_BLOCK, MLA_HEADS, MLA_NOPE), 1, 0)
    qp_b = jnp.moveaxis(q_pe.reshape(b, nb, Q_BLOCK, MLA_HEADS, MLA_ROPE), 1, 0)
    starts = jnp.arange(nb, dtype=jnp.int32) * Q_BLOCK

    def block(args):
        qn, qp, i0 = args
        sc = (jnp.einsum('bqhd,bkhd->bhqk', qn, k_nope)
              + jnp.einsum('bqhd,bkd->bhqk', qp, k_pe)).astype(jnp.float32) * scale
        q_chunk = (i0 + jnp.arange(Q_BLOCK)) // CHUNK_2
        mask = key_chunk[None, :] <= q_chunk[:, None]
        sc = jnp.where(mask, sc, -jnp.inf)
        p = jax.nn.softmax(sc, axis=-1).astype(v.dtype)
        return jnp.einsum('bhqk,bkhe->bqhe', p, v)

    out = lax.map(block, (qn_b, qp_b, starts))
    return jnp.moveaxis(out, 0, 1).reshape(b, s, MLA_WIDTH)

def gla(q, k, v, g_low, w_g2, b_g2):
    b, s, h, dk = q.shape
    dv = v.shape[-1]
    nc = s // CHUNK_2
    f32 = jnp.float32
    log_a = jax.nn.log_sigmoid((g_low @ w_g2 + b_g2).astype(f32)) / GLA_TAU
    cum = jnp.cumsum(log_a.reshape(b, nc, CHUNK_2, h, dk), axis=2)
    q = q.astype(f32).reshape(b, nc, CHUNK_2, h, dk)
    k = k.astype(f32).reshape(b, nc, CHUNK_2, h, dk) * (dk ** -0.5)
    v = v.astype(f32).reshape(b, nc, CHUNK_2, h, dv)
    e_pos = jnp.exp(cum)
    e_neg = jnp.exp(-cum)
    q_pos = q * e_pos
    past = jnp.einsum('bnihd,bnjhd->bnhij', q_pos, k * e_neg)
    fut = jnp.einsum('bnihd,bnjhd->bnhij', q * e_neg, k * e_pos)
    idx = jnp.arange(CHUNK_2)
    attn = jnp.where(idx[:, None] >= idx[None, :], past, fut)
    intra = jnp.einsum('bnhij,bnjhe->bnihe', attn, v)
    last = cum[:, :, -1]
    u = jnp.einsum('bnjhd,bnjhe->bnhde', k * jnp.exp(last[:, :, None] - cum), v)
    s_prev = chunk_states(u, jnp.exp(last))
    inter = jnp.einsum('bnihd,bnhde->bnihe', q_pos, s_prev)
    return (intra + inter).reshape(b, s, h, dv)

def second_inputs(seed: int = 0) -> dict:
    key = jax.random.key(seed)
    ks = jax.random.split(key, 16)
    f32 = jnp.float32

    def normal(k, shape, scale):
        return jax.random.normal(k, shape, f32) * scale

    def gain(k, shape):
        return 1.0 + 0.02 * jax.random.normal(k, shape, f32)

    x = normal(ks[0], (BATCH, SEQ, D_MODEL), 1.0)
    c = normal(ks[1], (BATCH, D_MODEL), 1.0)
    offset = jax.random.randint(ks[2], (BATCH, 1), 0, 4096, dtype=jnp.int32)
    positions = offset + jnp.arange(SEQ, dtype=jnp.int32)[None, :]
    norm_w = gain(ks[3], (DEPTH, D_MODEL))
    ada_w = normal(ks[4], (DEPTH, D_MODEL, 3 * D_MODEL), 0.5 * D_MODEL ** -0.5)
    ada_b = normal(ks[5], (DEPTH, 3 * D_MODEL), 0.02)
    w_in = normal(ks[6], (DEPTH, D_MODEL, IN_COLS), D_MODEL ** -0.5)
    mla_q_norm = gain(ks[7], (DEPTH, MLA_Q_RANK))
    w_uq = normal(ks[8], (DEPTH, MLA_Q_RANK, MLA_HEADS * (MLA_NOPE + MLA_ROPE)), MLA_Q_RANK ** -0.5)
    mla_kv_norm = gain(ks[9], (DEPTH, MLA_KV_RANK))
    w_ukv = normal(ks[10], (DEPTH, MLA_KV_RANK, MLA_HEADS * (MLA_NOPE + MLA_V)), MLA_KV_RANK ** -0.5)
    gla_w_g2 = normal(ks[11], (DEPTH, GLA_GATE_RANK, GLA_KWIDTH), GLA_GATE_RANK ** -0.5)
    gla_b_g2 = normal(ks[12], (DEPTH, GLA_KWIDTH), 0.02)
    gla_norm = gain(ks[13], (DEPTH, GLA_DV))
    w_out = normal(ks[14], (DEPTH, MIX_WIDTH, D_MODEL), MIX_WIDTH ** -0.5)
    final_norm = gain(ks[15], (D_MODEL,))
    return {"x": x, "c": c, "positions": positions, "norm_w": norm_w, "ada_w": ada_w,
            "ada_b": ada_b, "w_in": w_in, "mla_q_norm": mla_q_norm, "w_uq": w_uq,
            "mla_kv_norm": mla_kv_norm, "w_ukv": w_ukv, "gla_w_g2": gla_w_g2,
            "gla_b_g2": gla_b_g2, "gla_norm": gla_norm, "w_out": w_out,
            "final_norm": final_norm}

def second_block(x, c, positions, norm_w, ada_w, ada_b, w_in, mla_q_norm, w_uq, mla_kv_norm,
              w_ukv, gla_w_g2, gla_b_g2, gla_norm, w_out, final_norm):
    b, s, _ = x.shape
    c_act = jax.nn.silu(c)
    for l in range(DEPTH):
        shift, scale, gate = jnp.split(c_act @ ada_w[l] + ada_b[l], 3, axis=-1)
        h = rms_norm(x, norm_w[l]) * (1.0 + scale[:, None, :]) + shift[:, None, :]
        proj = h @ w_in[l]
        ret_p, mla_p, gla_p = split_cols(proj, (sum(RET_SPLIT), sum(MLA_SPLIT), sum(GLA_SPLIT)))

        rq, rk, rv, rz = split_cols(ret_p, RET_SPLIT)
        r_o = retention(rope(to_heads(rq, RET_HEADS), positions),
                        rope(to_heads(rk, RET_HEADS), positions),
                        to_heads(rv, RET_HEADS))
        r_o = rms_norm(r_o).astype(x.dtype).reshape(b, s, RET_WIDTH)

        mq, mkv, mkr, mz = split_cols(mla_p, MLA_SPLIT)
        m_o = mla(mq, mkv, mkr, mla_q_norm[l], w_uq[l], mla_kv_norm[l], w_ukv[l], positions)

        gq, gk, gv, gg, gz = split_cols(gla_p, GLA_SPLIT)
        g_o = gla(to_heads(gq, GLA_HEADS), to_heads(gk, GLA_HEADS), to_heads(gv, GLA_HEADS),
                  gg, gla_w_g2[l], gla_b_g2[l])
        g_o = rms_norm(g_o, gla_norm[l]).astype(x.dtype).reshape(b, s, GLA_WIDTH)

        mixed = jnp.concatenate([r_o * jax.nn.silu(rz), m_o * jax.nn.silu(mz),
                                 g_o * jax.nn.silu(gz)], axis=-1)
        x = x + gate[:, None, :] * (mixed @ w_out[l])
    return rms_norm(x, final_norm)


def setup_inputs(seed=0):
    out = dict(first_inputs(seed))
    for name, value in second_inputs(seed + 1).items():
        if name != "x":
            out[name + "_2"] = value
    return out


def reference(
    x, mem, mem_ln_g, mem_ln_b, w_mem_kv, router_w, router_b, na_w_in, na_rpb, ml_w_in,
    ml_conv_w, ml_conv_b, ml_w_qkv, ml_gate_b, ml_norm_g, ml_skip, w_out, ln_g, ln_b,
    exp_w_gate, exp_w_up, exp_w_down, c_2, positions_2, norm_w_2, ada_w_2, ada_b_2, w_in_2,
    mla_q_norm_2, w_uq_2, mla_kv_norm_2, w_ukv_2, gla_w_g2_2, gla_b_g2_2, gla_norm_2, w_out_2,
    final_norm_2,
):
    x = first_block(
        x, mem, mem_ln_g, mem_ln_b, w_mem_kv, router_w, router_b, na_w_in, na_rpb, ml_w_in,
        ml_conv_w, ml_conv_b, ml_w_qkv, ml_gate_b, ml_norm_g, ml_skip, w_out, ln_g, ln_b,
        exp_w_gate, exp_w_up, exp_w_down,
    )
    return second_block(
        x, c_2, positions_2, norm_w_2, ada_w_2, ada_b_2, w_in_2, mla_q_norm_2, w_uq_2,
        mla_kv_norm_2, w_ukv_2, gla_w_g2_2, gla_b_g2_2, gla_norm_2, w_out_2, final_norm_2,
    )


_drawn_inputs = setup_inputs


def setup_inputs(seed=0):
    import zlib

    import numpy as np

    out = dict(_drawn_inputs(seed))
    spreads = {}
    factors = {'mem_ln_g': 3.775,
     'mem_ln_b': 3.294,
     'na_rpb': 4.027,
     'ml_skip': 4.178,
     'norm_w_2': 6.975,
     'ada_b_2': 2.887,
     'mla_q_norm_2': 8.0,
     'w_uq_2': 2.735,
     'mla_kv_norm_2': 8.0,
     'gla_b_g2_2': 8.0,
     'gla_norm_2': 8.0,
     'final_norm_2': 2.885}
    for name, (base, spread) in spreads.items():
        noise = np.random.default_rng([zlib.crc32(name.encode()), seed]).standard_normal(out[name].shape)
        drawn = base * np.exp(spread * noise) if base else spread * noise
        out[name] = jnp.asarray(drawn.astype(out[name].dtype))
    for name, factor in factors.items():
        out[name] = (out[name] * factor).astype(out[name].dtype)
    return out
```

```python
from contextlib import contextmanager

import numpy as np

import concourse.bass as bass
from concourse import mybir

F32 = mybir.dt.float32
F32R = mybir.dt.float32r
I32 = mybir.dt.int32
U32 = mybir.dt.uint32
ALU = mybir.AluOpType
ACT = mybir.ActivationFunctionType
AX = mybir.AxisListType

P = 128
D = 1024
SEQ = 1024
TILES = SEQ // P
KT = D // P
BANK = 512
BANKS = 8
BIG = 1.0e30
LN_EPS = 1e-5
RMS_EPS = 1e-6
DEPTH = 2
ALPHA = (2 * DEPTH) ** 0.25

N_MEM = 256
MEM_HEADS = 4
HEAD = 64
MEM_W = MEM_HEADS * HEAD

NA_HEADS = 12
NA_W = NA_HEADS * HEAD
PAIRS = NA_HEADS // 2
GRID_W = 64
ROWS = SEQ // GRID_W
WIN_H = 8
WIN_W = 16
RPB_H = 2 * WIN_H - 1
RPB_W = 2 * WIN_W - 1

KB = 1024
BASE = 16512
AT_X = 0
AT_XT = 32 * KB
AT_WORK = 64 * KB
AT_CONST = 182 * KB


class Core:

    def __init__(self, io, mem):
        self.io, self.mem = io, mem


class Steps:

    def __init__(self, eng, sem):
        self.eng, self.sem, self.n = eng, sem, 0

    def mark(self, ins):
        ins.then_inc(self.sem, 1)
        self.n += 1

    def settle(self, ins):
        self.mark(ins)
        self.eng.wait_ge(self.sem, self.n)


@contextmanager
def stage(nc, *names):
    sems = [nc.alloc_semaphore(f"{n}_{nc.next_id()}") for n in names]
    with nc.Block() as block:
        yield block, dict(zip(names, sems))
    nc.clear_and_free_semaphores(sems)
    nc.all_engine_barrier()


class Memory:

    def __init__(self, nc):
        self.nc, self.n = nc, 0

    def at(self, name, offset, shape, dtype=F32):
        self.n += 1
        size = int(np.prod(shape[1:])) * 4
        assert offset + size <= 207 * KB, (name, offset, size)
        return self.nc.alloc_sbuf_tensor_at(f"{name}_{self.n}", list(shape), dtype, offset=BASE + offset)


RET_HEADS = 4
GLA_HEADS = 4
CHUNK_2 = 64
N_EXPERTS = 16


def constants():
    p = np.arange(P)
    j, i = np.meshgrid(p, p, indexing="ij")
    same = (i // CHUNK_2) == (j // CHUNK_2)
    t = {}
    t["ident"] = np.eye(P)
    t["ones"] = np.ones((P, P))
    t["fold"] = np.concatenate([np.eye(64), np.eye(64)], 0)
    t["before"] = (j < i)
    t["upto"] = (j <= i)
    t["from"] = (j >= i)
    t["chunk_upto"] = same & (j <= i)
    t["chunk_all"] = same
    t["chunk_of"] = np.stack([p < 64, p >= 64], 1)
    t["neg_future"] = np.where(j <= i, 0.0, -BIG)
    t["neg_past"] = np.where(j >= i, 0.0, -BIG)
    t["gla_past"] = same & (i >= j)
    t["gla_future"] = same & (i < j)
    gamma = 1.0 - 2.0 ** (-5.0 - np.arange(RET_HEADS))
    seen = same | (j < i)
    for h in range(RET_HEADS):
        t[f"decay{h}"] = np.where(seen, gamma[h] ** np.abs(i - j), 0.0) * 0.125
    t["ret_q"] = gamma[None, :] ** (p[:, None] + 1.0)
    t["ret_k"] = gamma[None, :] ** (P - 1.0 - p[:, None]) * 0.125
    half = 32
    inv = np.float32(10000.0) ** (-np.arange(half, dtype=np.float32) / np.float32(half))
    t["inv"] = np.broadcast_to(inv.astype(np.float32), (P, half))
    e = np.arange(16)
    t["first4"] = np.broadcast_to((e[None, :4] < e[:4, None]).reshape(1, 16), (P, 16))
    t["upto16"] = np.broadcast_to((e[None, :] <= e[:, None]).reshape(1, 256), (P, 256))
    t["caps"] = np.broadcast_to((np.arange(8) * float(P))[None, :], (P, 8))
    t["token"] = np.arange(8)[None, :] * float(P) + p[:, None]
    t["ret_carry"] = np.stack([np.where(p < 64, gamma[2 * pair] ** P, gamma[2 * pair + 1] ** P) for pair in range(2)], 1)
    t["early"] = np.broadcast_to((p < 64)[None, :] * 1.0, (P, P))
    t["late_big"] = np.broadcast_to((p >= 64)[None, :] * BIG, (P, P))
    t["eps_ln"] = np.full((P, 1), LN_EPS)
    t["eps_rms"] = np.full((P, 1), RMS_EPS)
    return {k: np.ascontiguousarray(v, dtype=np.float32) for k, v in t.items()}


CONSTS = constants()
CONST_COLS = sum(v.shape[1] for v in CONSTS.values())


def copy_out(eng, dst, src, scale=None):
    if eng.engine == mybir.EngineType.Activation:
        return eng.activation(dst, src, ACT.Copy, scale=1.0 if scale is None else scale)
    if scale is None:
        return eng.tensor_copy(dst, src)
    return eng.tensor_scalar(dst, src, scale, None, ALU.mult)


def rows_of(w):
    return w.rearrange("(k p) n -> p k n", p=P)


def take_high(eng, high, whole):
    return eng.tensor_copy(high, whole)


def leave_low(eng, low, whole, high):
    return eng.tensor_tensor(low, whole, high, ALU.subtract)


class Halves:

    def __init__(self, whole, low, high):
        self.whole, self.low, self.high, self.split = whole, low, high, False


def tiles_of(tile):
    return [tile[:, k, :] for k in range(tile.shape[1])]


def project(nc, core, chunks, slots, x, lows=None, highs=None):
    jobs = [(c, job) for c, (_, js) in enumerate(chunks) for job in js]
    ends = np.cumsum([len(js) for _, js in chunks])
    starts = ends - np.array([len(js) for _, js in chunks])
    split_x = highs is not None and not x.split
    with stage(nc, "weights_loaded0", "weights_loaded1", "products_ready", "even_emptied", "odd_emptied",
               "x_high", "x_low", "w_high", "w_low") as (block, s):
        loaded = [s["weights_loaded0"], s["weights_loaded1"]]
        emptied = [s["even_emptied"], s["odd_emptied"]]

        def slot(c, of=slots):
            shape = chunks[c][0].shape
            return of[c % 2][0:shape[0], 0:shape[1], 0:shape[2]]

        @block.sync
        def _(sp):
            for c, (view, _) in enumerate(chunks):
                if c >= 2:
                    sp.wait_ge(s["products_ready"], int(ends[c - 2]))
                sp.dma_start(slot(c), view).then_inc(loaded[c % 2], 16)

        @block.tensor
        def _(pe):
            for n, (c, (pairs, shape, _)) in enumerate(jobs):
                dst = core.bank[n % BANKS][0:shape[0], 0:shape[1]]
                if n >= BANKS:
                    pe.wait_ge(emptied[n % 2], (n - BANKS) // 2 + 1)
                if highs is None:
                    if n == starts[c]:
                        pe.wait_ge(loaded[c % 2], 16 * (c // 2 + 1))
                    ops = pairs(slot(c), x)
                    for m, (lhsT, rhs) in enumerate(ops):
                        mm = pe.matmul(dst, lhsT, rhs, start=(m == 0), stop=(m == len(ops) - 1))
                else:
                    if n == starts[c]:
                        pe.wait_ge(s["w_high"], c + 1)
                    if n == 0 and split_x:
                        pe.wait_ge(s["x_high"], len(x.high))
                    ops = pairs(slot(c, highs), x.high)
                    for m, (lhsT, rhs) in enumerate(ops):
                        pe.matmul(dst, lhsT, rhs, start=(m == 0), stop=False)
                    if n == starts[c]:
                        pe.wait_ge(s["w_low"], c + 1)
                    for lhsT, rhs in pairs(slot(c, lows), x.high):
                        pe.matmul(dst, lhsT, rhs, start=False, stop=False)
                    if n == 0 and split_x:
                        pe.wait_ge(s["x_low"], len(x.high))
                    for m, (lhsT, rhs) in enumerate(pairs(slot(c, highs), x.low)):
                        mm = pe.matmul(dst, lhsT, rhs, start=False, stop=(m == len(ops) - 1))
                mm.then_inc(s["products_ready"], 1)

        def empty(eng, parity, lo=0, hi=len(jobs)):
            for n in range(lo, hi):
                shape, out = jobs[n][1][1:]
                if n % 2 == parity:
                    eng.wait_ge(s["products_ready"], n + 1)
                    out(eng, core.bank[n % BANKS][0:shape[0], 0:shape[1]]).then_inc(emptied[parity], 1)

        @block.vector
        def _(dve):
            def split_weights(c):
                dve.wait_ge(loaded[c % 2], 16 * (c // 2 + 1))
                if c >= 2:
                    dve.wait_ge(s["products_ready"], int(ends[c - 2]))
                take_high(dve, slot(c, highs), slot(c)).then_inc(s["w_high"], 1)
                dve.wait_ge(s["w_high"], c + 1)
                leave_low(dve, slot(c, lows), slot(c), slot(c, highs)).then_inc(s["w_low"], 1)

            if highs is None:
                empty(dve, 0)
                return
            if split_x:
                for high, whole in zip(x.high, x.whole):
                    take_high(dve, high, whole).then_inc(s["x_high"], 1)
            split_weights(0)
            if split_x:
                dve.wait_ge(s["x_high"], len(x.high))
                for low, whole, high in zip(x.low, x.whole, x.high):
                    leave_low(dve, low, whole, high).then_inc(s["x_low"], 1)
            for c in range(len(chunks)):
                middle = int(starts[c]) + 2
                empty(dve, 0, int(starts[c]), middle)
                if c + 1 < len(chunks):
                    split_weights(c + 1)
                empty(dve, 0, middle, int(ends[c]))

        @block.scalar
        def _(act):
            empty(act, 1)
    if highs is not None:
        x.split = True


def transpose_rows(nc, core, src, dst, tiles=TILES, cols=KT):
    group = 4
    n_groups = tiles * cols // group
    with stage(nc, "blocks_ready", "even_emptied", "odd_emptied") as (block, s):
        emptied = [s["even_emptied"], s["odd_emptied"]]

        def where(n):
            return n // (cols // group), (n % (cols // group)) * group

        @block.tensor
        def _(pe):
            for n in range(n_groups):
                t, k0 = where(n)
                if n >= BANKS:
                    pe.wait_ge(emptied[n % 2], (n - BANKS) // 2 + 1)
                for k in range(group):
                    mm = pe.transpose(core.bank[n % BANKS][:, k * P:(k + 1) * P],
                                      src[:, t, (k0 + k) * P:(k0 + k + 1) * P], core.c["ident"])
                mm.then_inc(s["blocks_ready"], 1)

        def empty(eng, parity):
            for n in range(parity, n_groups, 2):
                t, k0 = where(n)
                eng.wait_ge(s["blocks_ready"], n + 1)
                copy_out(eng, dst[:, k0:k0 + group, t * P:(t + 1) * P],
                         core.bank[n % BANKS][:, :].rearrange("p (k q) -> p k q", k=group)).then_inc(emptied[parity], 1)

        @block.vector
        def _(dve):
            empty(dve, 0)

        @block.scalar
        def _(act):
            empty(act, 1)


def load_constants(nc, core):
    table = core.mem.at("consts", AT_CONST, [P, CONST_COLS])
    core.const_end = AT_CONST + (CONST_COLS * 4 + 63) // 64 * 64
    at = 0
    core.c = {}
    for name, v in CONSTS.items():
        core.c[name] = table[:, at:at + v.shape[1]]
        at += v.shape[1]
    with stage(nc, "loaded") as (block, s):
        @block.sync
        def _(sp):
            sp.dma_start(table[:, :], core.io["consts"]).then_inc(s["loaded"], 16)
            sp.wait_ge(s["loaded"], 16)


def broadcast_rows(row):
    return row.rearrange("(a n) -> a n", a=1).to_broadcast([P, row.shape[0]])


def moments(step, rows, stats, out):
    for h in range(2):
        step.mark(step.eng.bn_stats(stats[:, h, :], rows[:, h * BANK:(h + 1) * BANK]))
    step.eng.wait_ge(step.sem, step.n)
    step.mark(step.eng.bn_aggr(out, stats[:, :, :].rearrange("p a b -> p (a b)")))


def memory_rows(nc, core):
    m = core.mem
    T = N_MEM // P
    rows = m.at("mem_rows", AT_WORK, [P, T, D])
    rowsT = m.at("mem_rowsT", AT_WORK + 8 * KB, [P, KT, N_MEM])
    gain = m.at("mem_gain", AT_WORK + 16 * KB, [P, D])
    bias = m.at("mem_bias", AT_WORK + 20 * KB, [P, D])
    stats = m.at("mem_stats", AT_WORK + 24 * KB, [P, T, 2, 6])
    mv = m.at("mem_mv", AT_WORK + 25 * KB, [P, T, 2])
    rstd = m.at("mem_rstd", AT_WORK + 26 * KB, [P, T])
    with stage(nc, "rows_loaded", "steps", "variances", "deviations") as (block, s):
        @block.sync
        def _(sp):
            sp.dma_start(rows[:, :, :], core.io["mem"][0].rearrange("(t p) d -> p t d", p=P)).then_inc(s["rows_loaded"], 16)
            sp.dma_start(gain[:, :], broadcast_rows(core.io["mem_ln_g"])).then_inc(s["rows_loaded"], 16)
            sp.dma_start(bias[:, :], broadcast_rows(core.io["mem_ln_b"])).then_inc(s["rows_loaded"], 16)

        @block.scalar
        def _(act):
            act.wait_ge(s["variances"], 1)
            act.activation(rstd[:, :], mv[:, :, 1], ACT.Sqrt, bias=core.c["eps_ln"]).then_inc(s["deviations"], 1)

        @block.vector
        def _(dve):
            step = Steps(dve, s["steps"])
            dve.wait_ge(s["rows_loaded"], 48)
            for t in range(T):
                moments(step, rows[:, t, :], stats[:, t], mv[:, t, :])
            dve.wait_ge(s["steps"], step.n)
            dve.engine_nop().then_inc(s["variances"], 1)
            dve.wait_ge(s["deviations"], 1)
            step.settle(dve.reciprocal(rstd[:, :], rstd[:, :]))
            for t in range(T):
                step.settle(dve.tensor_scalar(rows[:, t, :], rows[:, t, :], mv[:, t, 0:1], rstd[:, t:t + 1], ALU.subtract, ALU.mult))
                step.settle(dve.tensor_tensor(rows[:, t, :], rows[:, t, :], gain[:, :], ALU.mult))
                step.settle(dve.tensor_tensor(rows[:, t, :], rows[:, t, :], bias[:, :], ALU.add))
    transpose_rows(nc, core, rows, rowsT, tiles=T)
    w = rows_of(core.io["w_mem_kv"])
    slots = [m.at(f"ring{i}", AT_WORK + (32 + 16 * i) * KB, [P, KT, BANK]) for i in range(2)]
    jobs = []
    for pair in range(2):
        jobs.append((lambda w, x, pair=pair: [(w[:, k, pair * P:(pair + 1) * P], x[k]) for k in range(KT)],
                     (P, N_MEM), lambda e, ps, pair=pair: copy_out(e, core.mem_kT[:, pair, :], ps)))
    for t in range(T):
        jobs.append((lambda w, x, t=t: [(x[k][:, t * P:(t + 1) * P], w[:, k, MEM_W:2 * MEM_W]) for k in range(KT)],
                     (P, MEM_W), lambda e, ps, t=t: copy_out(e, core.mem_v[:, t, :], ps)))
    project(nc, core, [(w, jobs)], slots, tiles_of(rowsT))


def feature_jobs(c0, n_tiles, width, out):
    jobs = []
    for n in range(n_tiles):
        for half in range(SEQ // BANK):
            jobs.append((
                lambda w, x, n=n, half=half: [(w[:, k, c0 + n * width:c0 + (n + 1) * width],
                                               x[k][:, half * BANK:(half + 1) * BANK]) for k in range(KT)],
                (width, BANK), lambda e, ps, n=n, half=half: out(e, ps, n, half)))
    return jobs


def token_jobs(c0, cols, out):
    return [(lambda w, x, t=t: [(x[k][:, t * P:(t + 1) * P], w[:, k, c0:c0 + cols]) for k in range(KT)],
             (P, cols), lambda e, ps, t=t: out(e, ps, t)) for t in range(TILES)]


def load_rows(nc, core, dst, src):
    with stage(nc, "loaded") as (block, s):
        @block.sync
        def _(sp):
            sp.dma_start(dst[:, :, :], src.rearrange("(t p) d -> p t d", p=P)).then_inc(s["loaded"], 16)
            sp.wait_ge(s["loaded"], 16)


def bias_table(nc, core, bias):
    span = 2 * GRID_W
    pad = core.rpb_pad
    zero = core.mem.at("rpb_zero", AT_WORK + 24 * KB, [NA_HEADS * RPB_H // 2, span])
    turned = core.mem.at("rpb_turned", AT_WORK, [P, PAIRS, RPB_H, GRID_W])
    with stage(nc, "zeroed", "zero_stored", "rows_stored", "loaded", "negated", "masked") as (block, s):
        @block.vector
        def _(dve):
            dve.memset(zero[0:90, :], 0.0).then_inc(s["zeroed"], 1)
            dve.wait_ge(s["loaded"], 16 * 2 * PAIRS)
            flat = "p a r c -> p (a r) c"
            dve.tensor_scalar(bias[:, :, :, :].rearrange(flat), turned[:, :, :, ::-1].rearrange(flat), -1.0, None,
                              ALU.mult).then_inc(s["negated"], 1)

        @block.sync
        def _(sp):
            sp.wait_ge(s["zeroed"], 1)
            flat = pad.rearrange("h r c -> (h r) c")
            for half in range(2):
                sp.dma_start(flat[90 * half:90 * half + 90, :], zero[0:90, :]).then_inc(s["zero_stored"], 16)
            sp.wait_ge(s["zero_stored"], 32)
            first = GRID_W - WIN_W
            sp.dma_start(pad[:, :, first:first + RPB_W], core.io["na_rpb"][0]).then_inc(s["rows_stored"], 16)
            sp.wait_ge(s["rows_stored"], 16)
            for h in range(NA_HEADS):
                side = (h % 2) * GRID_W
                src = bass.AP(tensor=pad.tensor, offset=pad.offset + h * RPB_H * span,
                              ap=[[1, GRID_W], [span, RPB_H], [1, GRID_W]])
                sp.dma_start(turned[side:side + GRID_W, h // 2, :, :], src).then_inc(s["loaded"], 16)

        @block.gpsimd
        def _(pool):
            pool.wait_ge(s["negated"], 1)
            step = Steps(pool, s["masked"])
            for side in range(2):
                p0 = side * GRID_W
                left = bias[p0:p0 + GRID_W, :, :, 0:GRID_W - WIN_W]
                step.mark(pool.affine_select(out=left, in_=left, compare_op=ALU.is_ge, fill=BIG, base=WIN_W // 2,
                                             pattern=[[0, PAIRS], [0, RPB_H], [1, GRID_W - WIN_W]], channel_multiplier=-1))
            pool.wait_ge(s["masked"], step.n)
            for side in range(2):
                p0 = side * GRID_W
                right = bias[p0:p0 + GRID_W, :, :, WIN_W:GRID_W]
                step.mark(pool.affine_select(out=right, in_=right, compare_op=ALU.is_ge, fill=BIG,
                                             base=WIN_W // 2 - 1 - WIN_W,
                                             pattern=[[0, PAIRS], [0, RPB_H], [-1, GRID_W - WIN_W]], channel_multiplier=1))


def neighbourhood(nc, core, qT, kT, v, v_odd, bias, mixT):
    m = core.mem
    units = [(r, pair) for r in range(ROWS) for pair in range(PAIRS)]
    U = len(units)
    KEYS = WIN_H * GRID_W
    NP = 3
    base = AT_WORK + 104 * KB
    probs = m.at("na_probs", base, [P, NP, KEYS])
    probsT = m.at("na_probsT", base + 6 * KB, [P, 2, KEYS])
    outs = m.at("na_outs", base + 10 * KB, [P, 2, P])
    low = m.at("na_low", base + 11 * KB, [P, U])
    sums = m.at("na_sums", base + 11 * KB + 512, [P, U])
    inv = m.at("na_inv", base + 12 * KB, [P, U])
    s_bank, t_bank, o_bank, f_bank = ([core.bank[i], core.bank[i + 1]] for i in (0, 2, 4, 6))

    def window(r):
        return min(max(r - WIN_H // 2, 0), ROWS - WIN_H)

    zero = m.at("zero_row", base + 13 * KB, [P, 256])
    pieces = core.expert_rows.rearrange("(b p) (c n) -> p b c n", p=P, n=256)
    with stage(nc, "zeroed", "rows_zeroed", "v_shifted", "outs_zeroed", "scores_ready", "biased", "probs_ready", "turned", "turned_copied", "values_ready",
               "inverted", "normed", "folded", "row_copied") as (block, s):
        @block.sync
        def _(sp):
            sp.dma_start(v_odd[0:64, 0:7, :], v[64:128, 0:7, :]).then_inc(s["v_shifted"], 16)
            sp.dma_start(v_odd[64:128, 0:7, :], v[0:64, 1:8, :]).then_inc(s["v_shifted"], 16)
            sp.wait_ge(s["zeroed"], 1)
            for b in range(pieces.shape[1]):
                sp.dma_start(pieces[:, b], zero[:, :].unsqueeze(1).to_broadcast([P, D // 256, 256])).then_inc(s["rows_zeroed"], 16)
            sp.wait_ge(s["rows_zeroed"], 16 * pieces.shape[1])

        @block.tensor
        def _(pe):
            def scores(u):
                r, pair = units[u]
                if u >= 2:
                    pe.wait_ge(s["biased"], u - 1)
                k0 = window(r) * GRID_W
                for side in range(2):
                    p0 = side * HEAD
                    mm = pe.matmul(s_bank[u % 2][p0:p0 + HEAD, :], qT[p0:p0 + HEAD, pair, r * GRID_W:(r + 1) * GRID_W],
                                   kT[p0:p0 + HEAD, pair, k0:k0 + KEYS], start=True, stop=True)
                mm.then_inc(s["scores_ready"], 1)

            def turn(u):
                pe.wait_ge(s["probs_ready"], u + 1)
                if u >= 2:
                    pe.wait_ge(s["turned_copied"], u - 1)
                for c in range(KEYS // P):
                    mm = pe.transpose(t_bank[u % 2][:, c * P:(c + 1) * P], probs[:, u % NP, c * P:(c + 1) * P], core.c["ident"])
                mm.then_inc(s["turned"], 1)

            def values(u):
                r, pair = units[u]
                pe.wait_ge(s["turned_copied"], u + 1)
                if u >= 2:
                    pe.wait_ge(s["normed"], u - 1)
                w0 = window(r)
                table, t0 = (v, w0 // 2) if w0 % 2 == 0 else (v_odd, w0 // 2)
                for side in range(2):
                    p0 = side * HEAD
                    h = 2 * pair + side
                    for c in range(KEYS // P):
                        mm = pe.matmul(o_bank[u % 2][p0:p0 + HEAD, p0:p0 + HEAD],
                                       probsT[:, u % 2, c * P + p0:c * P + p0 + HEAD],
                                       table[:, t0 + c, h * HEAD:(h + 1) * HEAD], start=(c == 0), stop=(c == KEYS // P - 1))
                mm.then_inc(s["values_ready"], 1)

            def fold(u):
                r, pair = units[u]
                pe.wait_ge(s["normed"], u + 1)
                if pair == 0 and r >= 2:
                    pe.wait_ge(s["row_copied"], r - 1)
                pe.matmul(f_bank[r % 2][:, pair * HEAD:(pair + 1) * HEAD], outs[:, u % 2, :], core.c["fold"],
                          start=True, stop=True).then_inc(s["folded"], 1)

            pe.wait_ge(s["v_shifted"], 32)
            for i in range(U + 3):
                if i < U:
                    scores(i)
                if 1 <= i < U + 1:
                    turn(i - 1)
                if 2 <= i < U + 2:
                    values(i - 2)
                if i >= 3:
                    fold(i - 3)

        @block.vector
        def _(dve):
            dve.memset(zero[:, :], 0.0).then_inc(s["zeroed"], 1)
            dve.memset(outs[:, :, :], 0.0).then_inc(s["outs_zeroed"], 1)
            dve.wait_ge(s["outs_zeroed"], 1)
            for i in range(U + 2):
                if i < U:
                    r, pair = units[i]
                    d0 = window(r) - r + WIN_H - 1
                    dve.wait_ge(s["scores_ready"], i + 1)
                    if i >= NP:
                        dve.wait_ge(s["turned"], i - NP + 1)
                    dve.tensor_tensor_reduce(probs[:, i % NP, :], s_bank[i % 2][:, :],
                                             bias[:, pair, d0:d0 + WIN_H, :].rearrange("p r c -> p (r c)"),
                                             1.0, 3.0e38, ALU.add, ALU.min, low[:, i:i + 1]).then_inc(s["biased"], 1)
                if i >= 2:
                    u = i - 2
                    dve.wait_ge(s["probs_ready"], u + 1)
                    dve.reciprocal(inv[:, u:u + 1], sums[:, u:u + 1]).then_inc(s["inverted"], 1)
                    dve.wait_ge(s["inverted"], u + 1)
                    dve.wait_ge(s["values_ready"], u + 1)
                    if u >= 2:
                        dve.wait_ge(s["folded"], u - 1)
                    for side in range(2):
                        q = slice(side * HEAD, (side + 1) * HEAD)
                        ins = dve.tensor_scalar(outs[q, u % 2, q], o_bank[u % 2][q, q], inv[q, u:u + 1], None, ALU.mult)
                    ins.then_inc(s["normed"], 1)

        @block.scalar
        def _(act):
            for i in range(U + 4):
                if i < U:
                    act.wait_ge(s["biased"], i + 1)
                    act.activation(probs[:, i % NP, :], probs[:, i % NP, :], ACT.Exp, bias=low[:, i:i + 1], scale=-1.0,
                                   accum_out=sums[:, i:i + 1]).then_inc(s["probs_ready"], 1)
                if 1 <= i < U + 1:
                    u = i - 1
                    act.wait_ge(s["turned"], u + 1)
                    if u >= 2:
                        act.wait_ge(s["values_ready"], u - 1)
                    act.activation(probsT[:, u % 2, :], t_bank[u % 2][:, :], ACT.Copy).then_inc(s["turned_copied"], 1)
                if i >= 4 and units[i - 4][1] == PAIRS - 1:
                    r = units[i - 4][0]
                    act.wait_ge(s["folded"], i - 3)
                    act.activation(mixT[:, 0:PAIRS, r * GRID_W:(r + 1) * GRID_W],
                                   f_bank[r % 2][:, 0:PAIRS * HEAD].rearrange("p (a q) -> p a q", a=PAIRS),
                                   ACT.Copy).then_inc(s["row_copied"], 1)


def memory_attention(nc, core, qT, outT):
    m = core.mem
    U = TILES
    base = AT_WORK
    probs = m.at("ma_probs", base, [P, 2, MEM_HEADS * N_MEM])
    probsT = m.at("ma_probsT", base + 8 * KB, [P, 2, MEM_HEADS * N_MEM])
    outs = m.at("ma_outs", base + 16 * KB, [P, 2, MEM_W])
    low = m.at("ma_low", base + 18 * KB, [P, U, MEM_HEADS])
    sums = m.at("ma_sums", base + 18 * KB + 256, [P, U, MEM_HEADS])
    inv = m.at("ma_inv", base + 18 * KB + 512, [P, U, MEM_HEADS])
    b = core.bank
    CH = N_MEM // P
    with stage(nc, "scores_ready", "lows_ready", "probs_ready", "turned", "turned_copied", "values_ready", "inverted",
               "normed", "out_turned", "out_copied") as (block, s):
        @block.tensor
        def _(pe):
            def scores(u):
                if u >= 1:
                    pe.wait_ge(s["probs_ready"], u)
                for h in range(MEM_HEADS):
                    p0 = (h % 2) * HEAD
                    mm = pe.matmul(b[h % 2][:, (h // 2) * N_MEM:(h // 2 + 1) * N_MEM],
                                   qT[p0:p0 + HEAD, h // 2, u * P:(u + 1) * P], core.mem_kT[p0:p0 + HEAD, h // 2, :],
                                   start=True, stop=True)
                mm.then_inc(s["scores_ready"], 1)

            def turn(u):
                pe.wait_ge(s["probs_ready"], u + 1)
                if u >= 1:
                    pe.wait_ge(s["turned_copied"], u)
                for c in range(MEM_HEADS * CH):
                    mm = pe.transpose(b[2 + c // 4][:, (c % 4) * P:(c % 4 + 1) * P], probs[:, u % 2, c * P:(c + 1) * P], core.c["ident"])
                mm.then_inc(s["turned"], 1)

            def values(u):
                pe.wait_ge(s["turned_copied"], u + 1)
                if u >= 2:
                    pe.wait_ge(s["normed"], u - 1)
                for h in range(MEM_HEADS):
                    for c in range(CH):
                        mm = pe.matmul(b[4 + u % 2][:, h * HEAD:(h + 1) * HEAD],
                                       probsT[:, u % 2, (h * CH + c) * P:(h * CH + c + 1) * P],
                                       core.mem_v[:, c, h * HEAD:(h + 1) * HEAD], start=(c == 0), stop=(c == CH - 1))
                mm.then_inc(s["values_ready"], 1)

            def turn_out(u):
                pe.wait_ge(s["normed"], u + 1)
                if u >= 2:
                    pe.wait_ge(s["out_copied"], u - 1)
                for c in range(MEM_W // P):
                    mm = pe.transpose(b[6 + u % 2][:, c * P:(c + 1) * P], outs[:, u % 2, c * P:(c + 1) * P], core.c["ident"])
                mm.then_inc(s["out_turned"], 1)

            for i in range(U + 3):
                if i < U:
                    scores(i)
                if 1 <= i < U + 1:
                    turn(i - 1)
                if 2 <= i < U + 2:
                    values(i - 2)
                if i >= 3:
                    turn_out(i - 3)

        @block.vector
        def _(dve):
            for i in range(U + 3):
                if i < U:
                    dve.wait_ge(s["scores_ready"], i + 1)
                    for n in range(2):
                        ins = dve.tensor_reduce(low[:, i, n:MEM_HEADS:2], b[n][:, :].rearrange("p (h k) -> p h k", h=2), AX.X, ALU.min)
                    ins.then_inc(s["lows_ready"], 1)
                if 2 <= i < U + 2:
                    u = i - 2
                    dve.wait_ge(s["probs_ready"], u + 1)
                    dve.reciprocal(inv[:, u, :], sums[:, u, :]).then_inc(s["inverted"], 1)
                    dve.wait_ge(s["inverted"], u + 1)
                    dve.wait_ge(s["values_ready"], u + 1)
                    if u >= 2:
                        dve.wait_ge(s["out_turned"], u - 1)
                    dve.tensor_tensor(outs[:, u % 2, :].rearrange("p (h d) -> p h d", h=MEM_HEADS),
                                      b[4 + u % 2][:, 0:MEM_W].rearrange("p (h d) -> p h d", h=MEM_HEADS),
                                      inv[:, u, :].unsqueeze(2).to_broadcast([P, MEM_HEADS, HEAD]), ALU.mult).then_inc(s["normed"], 1)
                if i >= 3:
                    u = i - 3
                    dve.wait_ge(s["out_turned"], u + 1)
                    dve.tensor_copy(outT[:, :, u * P:(u + 1) * P],
                                    b[6 + u % 2][:, 0:MEM_W].rearrange("p (c q) -> p c q", q=P)).then_inc(s["out_copied"], 1)

        @block.scalar
        def _(act):
            for i in range(U + 1):
                if i < U:
                    act.wait_ge(s["lows_ready"], i + 1)
                    if i >= 2:
                        act.wait_ge(s["turned"], i - 1)
                    for h in range(MEM_HEADS):
                        ins = act.activation(probs[:, i % 2, h * N_MEM:(h + 1) * N_MEM], b[h % 2][:, (h // 2) * N_MEM:(h // 2 + 1) * N_MEM],
                                             ACT.Exp, bias=low[:, i, h:h + 1], scale=-1.0, accum_out=sums[:, i, h:h + 1])
                    ins.then_inc(s["probs_ready"], 1)
                if i >= 1:
                    u = i - 1
                    act.wait_ge(s["turned"], u + 1)
                    if u >= 2:
                        act.wait_ge(s["values_ready"], u - 1)
                    for n in range(2):
                        ins = act.activation(probsT[:, u % 2, n * BANK:(n + 1) * BANK], b[2 + n][:, :], ACT.Copy)
                    ins.then_inc(s["turned_copied"], 1)


def ring(core, cols):
    size = KT * cols * 4
    return ([core.mem.at(f"ring{i}", AT_WORK + i * size, [P, KT, cols]) for i in range(2)],
            [core.mem.at(f"ring_low{i}", AT_WORK + i * size, [P, KT, cols], F32R) for i in range(2)],
            [core.mem.at(f"ring_high{i}", AT_WORK + (2 + i) * size, [P, KT, cols], F32R) for i in range(2)])


def na_layer(nc, core):
    m = core.mem
    xT = m.at("na_xT", AT_XT, [P, KT, SEQ])
    x = m.at("na_x", AT_X, [P, TILES, D])
    load_rows(nc, core, x, core.io["x"][0])
    transpose_rows(nc, core, x, xT)
    qm = m.at("na_qm", AT_X + 23 * KB, [P, 2, SEQ])
    qT = m.at("na_qT", AT_WORK + 32 * KB, [P, PAIRS, SEQ])
    kT = m.at("na_kT", AT_WORK + 56 * KB, [P, PAIRS, SEQ])
    v = m.at("na_v", AT_WORK + 80 * KB, [P, TILES, NA_W])
    high_a = m.at("na_x_high", AT_X, [P, 5, SEQ], F32R)
    low = m.at("na_x_low", AT_XT, [P, KT, SEQ], F32R)
    high_b = m.at("na_x_high", AT_WORK + 104 * KB, [P, 3, SEQ], F32R)
    w = rows_of(core.io["na_w_in"][0])
    scale = -(HEAD ** -0.5)
    cols = 2 * P

    def qk_out(c):
        def out(e, ps, n, half):
            tile = c * 2 + n
            dst = (qT[:, tile] if tile < PAIRS else kT[:, tile - PAIRS])[:, half * BANK:(half + 1) * BANK]
            return copy_out(e, dst, ps, scale if tile < PAIRS else None)
        return out

    def v_out(c):
        return lambda e, ps, t: copy_out(e, v[:, t, c * cols:(c + 1) * cols], ps)

    views = [w[:, :, c * cols:(c + 1) * cols] for c in range(10)]
    chunks = [(views[c], feature_jobs(0, 2, P, qk_out(c))) for c in range(6)]
    chunks += [(views[6 + c], token_jobs(0, cols, v_out(c))) for c in range(3)]
    chunks.append((views[9], feature_jobs(0, 2, P, lambda e, ps, n, half: copy_out(e, qm[:, n, half * BANK:(half + 1) * BANK], ps, scale))))
    slots, lows, highs = ring(core, cols)
    project(nc, core, chunks, slots, Halves(tiles_of(xT), tiles_of(low), tiles_of(high_a) + tiles_of(high_b)), lows, highs)
    bias = m.at("na_bias", AT_X, [P, PAIRS, RPB_H, GRID_W])
    bias_table(nc, core, bias)
    mixT = m.at("mixT", AT_XT, [P, KT, SEQ])
    v_odd = m.at("na_v_odd", AT_WORK, [P, 7, NA_W])
    neighbourhood(nc, core, qT, kT, v, v_odd, bias, mixT)
    memory_attention(nc, core, qm, mixT[:, PAIRS:KT, :])
    return mixT


def const_table():
    return np.concatenate([CONSTS[k] for k in CONSTS], axis=1)


def make_core(nc, io):
    core = Core(io, Memory(nc))
    core.psum = nc.alloc_psum_tensor("psum", [P, BANKS, BANK], F32)
    core.bank = [core.psum[:, i, :] for i in range(BANKS)]
    core.rpb_pad = nc.dram_tensor("rpb_pad", (NA_HEADS, RPB_H, 2 * GRID_W), F32, kind="Internal").ap()
    core.slot_ids = nc.dram_tensor("slot_ids", (34 * P, 1), U32, kind="Internal").ap()
    core.token_rows = nc.dram_tensor("token_rows", (SEQ, D), F32, kind="Internal").ap()
    core.expert_rows = nc.dram_tensor("expert_rows", (32 * P, D), F32, kind="Internal").ap()
    core.gate_rows = nc.dram_tensor("gate_rows", (96, 8, SEQ), F32, kind="Internal").ap()
    load_constants(nc, core)
    core.mem_kT = core.mem.at("mem_kT", core.const_end, [P, 2, N_MEM])
    core.mem_v = core.mem.at("mem_v", core.const_end + 2 * KB, [P, N_MEM // P, MEM_W])
    core.const_end += 4 * KB
    core.cos = core.mem.at("cos", core.const_end + 2 * KB, [P, TILES, 32])
    core.sin = core.mem.at("sin", core.const_end + 3 * KB, [P, TILES, 32])
    return core



N_GROUPS = 4
PER_GROUP = 4
TOP_K = 2
D_EXPERT = 512
MAX_BLOCKS = SEQ * TOP_K // P + N_EXPERTS
HT = D_EXPERT // P


class Modulation:
    CHUNKS = 6
    SEMAPHORES = ("ada_loaded", "ada_chunk0", "ada_chunk1", "c_ready", "ada_products", "ada_copied", "mod_steps")

    def __init__(self, core, l):
        m = core.mem
        o = core.const_end + 8 * KB + l * 512
        self.core, self.l = core, l
        self.c_col = m.at("c_col", o, [P, KT])
        self.b_col = m.at("ada_b_col", o + 32, [P, 2 * KT])
        self.w_col = m.at("norm_w_col", o + 96, [P, KT])
        self.cols = m.at("mod_cols", o + 128, [P, 2 * KT])
        self.shift, self.scale = self.cols[:, 0:KT], self.cols[:, KT:2 * KT]
        self.gate = m.at("gate", core.const_end + (4 if l == 0 else -4) * KB, [P, D])
        self.gate_b = m.at("gate_b", AT_WORK + 96 * KB, [P, D])
        self.slots = [m.at(f"ada{i}", AT_WORK + (64 + 16 * i) * KB, [P, KT, BANK]) for i in range(2)]
        self.col_bank, self.gate_banks = core.bank[5][:, 0:2 * KT], core.psum[:, 6:8, :]

    def load(self, eng, s):
        io, l = self.core.io, self.l
        with eng.bass.allow_non_contiguous_dma(reason="a few values a partition"):
            eng.dma_start(self.c_col[:, :], io["c_2"][0].rearrange("(k p) -> p k", p=P)).then_inc(s["ada_loaded"], 16)
            eng.dma_start(self.b_col[:, :], io["ada_b_2"][l, 0:2 * D].rearrange("(k p) -> p k", p=P)).then_inc(s["ada_loaded"], 16)
            eng.dma_start(self.w_col[:, :], io["norm_w_2"][l].rearrange("(k p) -> p k", p=P)).then_inc(s["ada_loaded"], 16)
        eng.dma_start(self.gate_b[:, :], broadcast_rows(io["ada_b_2"][l, 2 * D:3 * D])).then_inc(s["ada_loaded"], 16)
        for c in range(self.CHUNKS):
            if c >= 2:
                eng.wait_ge(s["ada_products"], c - 1)
            eng.dma_start(self.slots[c % 2][:, :, :], rows_of(io["ada_w_2"][l])[:, :, c * BANK:(c + 1) * BANK]).then_inc(s[f"ada_chunk{c % 2}"], 16)

    def product(self, pe, s, c):
        w = self.slots[c % 2]
        pe.wait_ge(s["c_ready"], 1)
        pe.wait_ge(s[f"ada_chunk{c % 2}"], 16 * (c // 2 + 1))
        if c < 4:
            for n in range(4):
                for k in range(KT):
                    mm = pe.matmul(self.col_bank[:, 4 * c + n:4 * c + n + 1], w[:, k, n * P:(n + 1) * P], self.c_col[:, k:k + 1],
                                   start=(k == 0), stop=(k == KT - 1))
        else:
            for k in range(KT):
                mm = pe.matmul(self.gate_banks[:, c - 4, :], self.c_col[:, k:k + 1].to_broadcast([P, P]), w[:, k, :],
                               start=(k == 0), stop=(k == KT - 1))
        mm.then_inc(s["ada_products"], 1)

    def activate(self, act, s):
        act.wait_ge(s["ada_loaded"], 64)
        act.activation(self.c_col[:, :], self.c_col[:, :], ACT.Silu).then_inc(s["c_ready"], 1)

    def finish(self, dve, s):
        step = Steps(dve, s["mod_steps"])
        dve.wait_ge(s["ada_products"], self.CHUNKS)
        step.mark(dve.tensor_tensor(self.gate[:, :], self.gate_banks.rearrange("p b n -> p (b n)"), self.gate_b[:, :], ALU.add))
        step.settle(dve.tensor_tensor(self.cols[:, :], self.col_bank, self.b_col[:, :], ALU.add))
        step.mark(dve.scalar_tensor_tensor(out=self.scale, in0=self.scale, scalar=1.0, in1=self.w_col[:, :], op0=ALU.add, op1=ALU.mult))


def residual_norm(nc, core, x, xT, gain, bias, parts=None, weights=None, experts=None, spill=None, beside=None):
    m = core.mem
    top = core.const_end
    stats = m.at("ln_stats", top, [P, TILES, 2, 6])
    mv = m.at("ln_mv", top + 512, [P, TILES, 2])
    rstd = m.at("ln_rstd", top + 640, [P, TILES])
    shift = m.at("ln_shift", top + 704, [P, TILES])
    g_rows = m.at("ln_gain", AT_WORK + 104 * KB, [P, D])
    b_rows = m.at("ln_bias", AT_WORK + 108 * KB, [P, D])
    HALVES = D // BANK
    t_banks = 5 if beside else BANKS
    with stage(nc, "vectors_loaded", "weights_loaded", *[f"rows_gathered{t}" for t in range(TILES)], "products_ready", "summed", "measured", "variance_ready",
               "deviation_ready", "inverted", "shift_ready", "normed", "gained", "rows_done", "rows_stored",
               "turned", "even_emptied", "odd_emptied", *(Modulation.SEMAPHORES if beside else ())) as (block, s):
        gathered = [s[f"rows_gathered{t}"] for t in range(TILES)]

        @block.sync
        def _(sp):
            if parts:
                for view, dst in weights:
                    sp.dma_start(dst, view).then_inc(s["weights_loaded"], 16)
            sp.dma_start(g_rows[:, :], broadcast_rows(gain)).then_inc(s["vectors_loaded"], 16)
            sp.dma_start(b_rows[:, :], broadcast_rows(bias)).then_inc(s["vectors_loaded"], 16)
            if beside:
                beside.load(sp, s)
            if spill is not None:
                for t in range(TILES):
                    sp.wait_ge(s["rows_done"], t + 1)
                    sp.dma_start(spill[t * P:(t + 1) * P, :], x[:, t, :]).then_inc(s["rows_stored"], 16)
                sp.wait_ge(s["rows_stored"], 16 * TILES)

        @block.tensor
        def _(pe):
            if parts:
                pe.wait_ge(s["weights_loaded"], 16 * len(weights))
                for n in range(TILES * HALVES):
                    t, half = divmod(n, HALVES)
                    if n >= BANKS:
                        pe.wait_ge(s["summed"], n - BANKS + 1)
                    for k, (left, right) in enumerate(parts):
                        mm = pe.matmul(core.bank[n % BANKS][:, :], left[:, t * P:(t + 1) * P],
                                       right[:, half * BANK:(half + 1) * BANK], start=(k == 0), stop=(k == len(parts) - 1))
                    mm.then_inc(s["products_ready"], 1)
                pe.wait_ge(s["summed"], TILES * HALVES)
            for n in range(TILES * 2):
                t, k0 = n // 2, (n % 2) * 4
                if beside and n % 2 == 0 and t < beside.CHUNKS:
                    beside.product(pe, s, t)
                if xT is None:
                    continue
                if n % 2 == 0:
                    pe.wait_ge(s["rows_done"], t + 1)
                if n >= t_banks:
                    before = n - t_banks
                    pe.wait_ge([s["even_emptied"], s["odd_emptied"]][before % 2], before // 2 + 1)
                for k in range(4):
                    mm = pe.transpose(core.bank[n % t_banks][:, k * P:(k + 1) * P], x[:, t, (k0 + k) * P:(k0 + k + 1) * P],
                                      core.c["ident"])
                mm.then_inc(s["turned"], 1)

        @block.vector
        def _(dve):
            summed = Steps(dve, s["summed"])
            measured = Steps(dve, s["measured"])
            inverted = Steps(dve, s["inverted"])
            shifted = Steps(dve, s["shift_ready"])
            dve.wait_ge(s["vectors_loaded"], 32)
            for i in range(TILES + 1):
                if i < TILES:
                    if parts:
                        for half in range(HALVES):
                            cols = slice(half * BANK, (half + 1) * BANK)
                            dve.wait_ge(s["products_ready"], i * HALVES + half + 1)
                            summed.mark(dve.scalar_tensor_tensor(out=x[:, i, cols], in0=x[:, i, cols], scalar=ALPHA,
                                                                 in1=core.bank[(i * HALVES + half) % BANKS][:, :],
                                                                 op0=ALU.mult, op1=ALU.add))
                    else:
                        slots, w, bufs = experts
                        summed.settle(dve.tensor_scalar(x[:, i, :], x[:, i, :], ALPHA, None, ALU.mult))
                        for k in range(TOP_K):
                            dve.wait_ge(gathered[i], 16 * TOP_K)
                            summed.settle(dve.scalar_tensor_tensor(out=x[:, i, :], in0=bufs[:, i, k, :], scalar=w[:, k, i:i + 1],
                                                                   in1=x[:, i, :], op0=ALU.mult, op1=ALU.add))
                    dve.wait_ge(s["summed"], summed.n)
                    for h in range(2):
                        measured.mark(dve.bn_stats(stats[:, i, h, :], x[:, i, h * BANK:(h + 1) * BANK]))
                    dve.wait_ge(s["measured"], measured.n)
                    dve.bn_aggr(mv[:, i, :], stats[:, i].rearrange("p a b -> p (a b)")).then_inc(s["variance_ready"], 1)
                if i >= 1:
                    t = i - 1
                    dve.wait_ge(s["deviation_ready"], t + 1)
                    inverted.settle(dve.reciprocal(rstd[:, t:t + 1], rstd[:, t:t + 1]))
                    shifted.mark(dve.scalar_tensor_tensor(out=shift[:, t:t + 1], in0=mv[:, t, 0:1], scalar=-1.0,
                                                          in1=rstd[:, t:t + 1], op0=ALU.mult, op1=ALU.mult))
                    dve.wait_ge(s["normed"], t + 1)
                    dve.tensor_tensor(x[:, t, :], x[:, t, :], g_rows[:, :], ALU.mult).then_inc(s["gained"], 1)
            for n in range(0, TILES * 2 if xT is not None else 0, 2):
                dve.wait_ge(s["turned"], n + 1)
                dve.tensor_copy(xT[:, 0:4, (n // 2) * P:(n // 2 + 1) * P],
                                core.bank[n % t_banks][:, :].rearrange("p (k q) -> p k q", k=4)).then_inc(s["even_emptied"], 1)
            if beside:
                beside.finish(dve, s)

        @block.scalar
        def _(act):
            if beside:
                beside.activate(act, s)
            for t in range(TILES):
                act.wait_ge(s["variance_ready"], t + 1)
                act.activation(rstd[:, t:t + 1], mv[:, t, 1:2], ACT.Sqrt, bias=core.c["eps_ln"]).then_inc(s["deviation_ready"], 1)
                act.wait_ge(s["shift_ready"], t + 1)
                act.activation(x[:, t, :], x[:, t, :], ACT.Identity, bias=shift[:, t:t + 1], scale=rstd[:, t:t + 1]).then_inc(s["normed"], 1)
            for n in range(1, TILES * 2 if xT is not None else 0, 2):
                act.wait_ge(s["turned"], n + 1)
                act.activation(xT[:, 4:8, (n // 2) * P:(n // 2 + 1) * P],
                               core.bank[n % t_banks][:, :].rearrange("p (k q) -> p k q", k=4), ACT.Copy).then_inc(s["odd_emptied"], 1)

        @block.gpsimd
        def _(pool):
            def gather(t):
                slots, w, bufs = experts
                for k in range(TOP_K):
                    pool.indirect_dma_start(out=bufs[:, t, k, :], out_offset=None, in_=core.expert_rows[:, :],
                                            in_offset=bass.IndirectOffsetOnAxis(ap=slots[:, k, t:t + 1], axis=0)
                                            ).then_inc(gathered[t], 16)
            if experts:
                for t in range(TILES):
                    gather(t)
            for t in range(TILES):
                pool.wait_ge(s["gained"], t + 1)
                pool.tensor_tensor(x[:, t, :], x[:, t, :], b_rows[:, :], ALU.add).then_inc(s["rows_done"], 1)


def expert_parts(core, layer):
    slots = [[core.mem.at(f"w_{part}{i}", AT_WORK + (48 * i + 16 * j) * KB, [P, HT if part == "down" else KT, D if part == "down" else BANK])
              for j, part in enumerate(("gate", "up", "down"))] for i in range(2)]
    srcs = [rows_of(core.io[f"exp_w_{part}"][layer].rearrange("e k n -> (e k) n")) for part in ("gate", "up", "down")]
    return slots, srcs, [KT, KT, HT]


def load_expert(sp, parts, e, sem):
    slots, srcs, n_k = parts
    for j in range(3):
        sp.dma_start(slots[e % 2][j][:, :, :], srcs[j][:, e * n_k[j]:(e + 1) * n_k[j], :]).then_inc(sem, 16)


def moe(nc, core, layer, x, xT):
    m = core.mem
    o = AT_WORK + 96 * KB
    top = core.const_end + 1 * KB
    slots = m.at("moe_slots", top, [P, TOP_K, TILES], U32)
    wts = m.at("moe_weights", top + 64, [P, TOP_K, TILES])
    ids = m.at("moe_ids", top + 128, [P, MAX_BLOCKS + 2], U32)
    bounds = m.at("moe_bounds", top + 384, [P, 2, N_EXPERTS], I32)
    parts = expert_parts(core, layer)
    loaded = [nc.alloc_semaphore(f"expert_loaded{i}_{layer}") for i in range(2)]
    route(nc, core, x, xT, slots, wts, ids, bounds, parts, loaded[0])
    run_experts(nc, core, ids, bounds, parts, loaded)
    nc.clear_and_free_semaphores(loaded)
    nc.all_engine_barrier()
    bufs = m.at("moe_gathered", AT_WORK, [P, TILES, TOP_K, D])
    return slots, wts, bufs


def route(nc, core, x, xT, slots, wts, ids, bounds, parts, first_loaded):
    m = core.mem
    TE = TILES * N_EXPERTS
    TG = TILES * N_GROUPS
    n = [0]

    def tmp(shape, dtype=F32):
        size = int(np.prod(shape[1:])) * 4
        out = m.at("route", AT_WORK + 96 * KB + n[0], shape, dtype)
        n[0] += (size + 63) // 64 * 64
        return out
    rw = tmp([P, KT, N_EXPERTS])
    rb = tmp([P, N_EXPERTS])
    scores = tmp([P, TE])
    biased = tmp([P, TE])
    gt = tmp([P, TG * 16])
    eq = tmp([P, TG * 16])
    rank = tmp([P, TE])
    two = tmp([P, TE])
    gsc = tmp([P, TG])
    ggt = tmp([P, TG * 4])
    geq = tmp([P, TG * 4])
    grank = tmp([P, TG])
    won = tmp([P, TG])
    sel = tmp([P, TOP_K, TE])
    both = tmp([P, TE])
    raw = tmp([P, TOP_K, TILES])
    total = tmp([P, TILES])
    offs = tmp([P, TILES + 1, N_EXPERTS])
    over = tmp([P, N_EXPERTS, 8])
    need = tmp([P, N_EXPERTS])
    pref = tmp([P, N_EXPERTS, N_EXPERTS])
    ends = tmp([P, N_EXPERTS])
    starts = tmp([P, N_EXPERTS])
    place = tmp([P, TE])
    pick = tmp([P, TOP_K, TE])
    slotf = tmp([P, TOP_K, TILES])
    zero = tmp([P, MAX_BLOCKS + 2], U32)
    token = tmp([P, TILES], U32)
    b = core.bank
    te = "p (t e) -> p t e"
    with stage(nc, "loaded", "logits_ready", "scores_ready", "steps", "chosen", "counts_ready", "placed", "zeroed", "ids_zeroed",
               "ids_stored", "ids_loaded") as (block, s):
        @block.sync
        def _(sp):
            sp.dma_start(rw[:, :, :], rows_of(core.io["router_w"])).then_inc(s["loaded"], 16)
            sp.dma_start(rb[:, :], broadcast_rows(core.io["router_b"])).then_inc(s["loaded"], 16)
            load_expert(sp, parts, 0, first_loaded)
            sp.wait_ge(s["zeroed"], 1)
            sp.dma_start(core.slot_ids.rearrange("(p b) a -> p (b a)", p=P), zero[:, :]).then_inc(s["ids_zeroed"], 16)
            sp.wait_ge(s["ids_stored"], 16 * TILES * TOP_K)
            with nc.allow_non_contiguous_dma(reason="one index per partition"):
                sp.dma_start(ids[:, :], core.slot_ids.rearrange("(b p) a -> p (b a)", p=P)).then_inc(s["ids_loaded"], 16)
            sp.wait_ge(s["ids_loaded"], 16)

        @block.tensor
        def _(pe):
            pe.wait_ge(s["loaded"], 32)
            for t in range(TILES):
                for k in range(KT):
                    mm = pe.matmul(b[0][:, t * 16:(t + 1) * 16], xT[:, k, t * P:(t + 1) * P], rw[:, k, :], start=(k == 0), stop=(k == KT - 1))
            mm.then_inc(s["logits_ready"], 1)
            pe.wait_ge(s["chosen"], 1)
            pe.matmul(b[1][:, 0:TE], core.c["before"], both[:, :], start=True, stop=True)
            pe.matmul(b[2][:, 0:TE], core.c["ones"], both[:, :], start=True, stop=True).then_inc(s["counts_ready"], 1)

        @block.scalar
        def _(act):
            act.wait_ge(s["logits_ready"], 1)
            act.activation(scores[:, :], b[0][:, 0:TE], ACT.Sigmoid).then_inc(s["scores_ready"], 1)

        @block.vector
        def _(dve):
            step = Steps(dve, s["steps"])
            dve.memset(zero[:, :], 0).then_inc(s["zeroed"], 1)
            step.mark(dve.tensor_copy(token[:, :], core.c["token"]))
            dve.wait_ge(s["loaded"], 32)
            dve.wait_ge(s["scores_ready"], 1)
            step.settle(dve.tensor_tensor(biased[:, :].rearrange(te, e=16), scores[:, :].rearrange(te, e=16),
                                          rb[:, :].unsqueeze(1).to_broadcast([P, TILES, 16]), ALU.add))
            b4 = biased[:, :].rearrange("p (g e) -> p g e", e=4)
            mine = b4.unsqueeze(3).to_broadcast([P, TG, 4, 4])
            other = b4.unsqueeze(2).to_broadcast([P, TG, 4, 4])
            q4 = "p (g a b) -> p g a b"
            step.mark(dve.tensor_tensor(gt[:, :].rearrange(q4, a=4, b=4), other, mine, ALU.is_gt))
            step.settle(dve.tensor_tensor(eq[:, :].rearrange(q4, a=4, b=4), other, mine, ALU.is_equal))
            first = core.c["first4"].unsqueeze(1).to_broadcast([P, TG, 16])
            step.settle(dve.tensor_tensor(eq[:, :].rearrange("p (g c) -> p g c", c=16), eq[:, :].rearrange("p (g c) -> p g c", c=16), first, ALU.mult))
            step.settle(dve.tensor_tensor(gt[:, :], gt[:, :], eq[:, :], ALU.add))
            step.settle(dve.tensor_reduce(rank[:, :], gt[:, :].rearrange("p (c b) -> p c b", b=4), AX.X, ALU.add))
            step.settle(dve.tensor_scalar(two[:, :], rank[:, :], 1.5, None, ALU.is_lt))
            step.settle(dve.tensor_tensor(two[:, :], two[:, :], biased[:, :], ALU.mult))
            step.settle(dve.tensor_reduce(gsc[:, :], two[:, :].rearrange("p (g e) -> p g e", e=4), AX.X, ALU.add))
            g4 = gsc[:, :].rearrange("p (t g) -> p t g", g=4)
            mine = g4.unsqueeze(3).to_broadcast([P, TILES, 4, 4])
            other = g4.unsqueeze(2).to_broadcast([P, TILES, 4, 4])
            step.mark(dve.tensor_tensor(ggt[:, :].rearrange(q4, a=4, b=4), other, mine, ALU.is_gt))
            step.settle(dve.tensor_tensor(geq[:, :].rearrange(q4, a=4, b=4), other, mine, ALU.is_equal))
            first = core.c["first4"].unsqueeze(1).to_broadcast([P, TILES, 16])
            step.settle(dve.tensor_tensor(geq[:, :].rearrange("p (g c) -> p g c", c=16), geq[:, :].rearrange("p (g c) -> p g c", c=16), first, ALU.mult))
            step.settle(dve.tensor_tensor(ggt[:, :], ggt[:, :], geq[:, :], ALU.add))
            step.settle(dve.tensor_reduce(grank[:, :], ggt[:, :].rearrange("p (c b) -> p c b", b=4), AX.X, ALU.add))
            step.settle(dve.tensor_scalar(won[:, :], grank[:, :], 0.5, None, ALU.is_lt))
            win = won[:, :].unsqueeze(2).to_broadcast([P, TG, 4])
            ge = "p (g e) -> p g e"
            for k in range(TOP_K):
                step.settle(dve.tensor_scalar(sel[:, k, :], rank[:, :], float(k), None, ALU.is_equal))
                step.settle(dve.tensor_tensor(sel[:, k, :].rearrange(ge, e=4), sel[:, k, :].rearrange(ge, e=4), win, ALU.mult))
            dve.tensor_tensor(both[:, :], sel[:, 0, :], sel[:, 1, :], ALU.add).then_inc(s["chosen"], 1)
            for k in range(TOP_K):
                step.settle(dve.tensor_tensor(pick[:, k, :], sel[:, k, :], scores[:, :], ALU.mult))
                step.settle(dve.tensor_reduce(raw[:, k, :], pick[:, k, :].rearrange(te, e=16), AX.X, ALU.add))
            step.settle(dve.tensor_tensor(total[:, :], raw[:, 0, :], raw[:, 1, :], ALU.add))
            step.settle(dve.reciprocal(total[:, :], total[:, :]))
            for k in range(TOP_K):
                step.mark(dve.tensor_tensor(wts[:, k, :], raw[:, k, :], total[:, :], ALU.mult))
            step.settle(dve.memset(offs[:, 0, :], 0.0))
            dve.wait_ge(s["counts_ready"], 1)
            for t in range(TILES):
                step.settle(dve.tensor_tensor(offs[:, t + 1, :], offs[:, t, :], b[2][:, t * 16:(t + 1) * 16], ALU.add))
            step.settle(dve.tensor_tensor(over[:, :, :], offs[:, TILES, :].unsqueeze(2).to_broadcast([P, 16, 8]),
                                          core.c["caps"].unsqueeze(1).to_broadcast([P, 16, 8]), ALU.is_gt))
            step.settle(dve.tensor_reduce(need[:, :], over[:, :, :], AX.X, ALU.add))
            step.settle(dve.tensor_scalar(need[:, :], need[:, :], 1.0, None, ALU.max))
            step.settle(dve.tensor_tensor(pref[:, :, :], core.c["upto16"].rearrange("p (a b) -> p a b", a=16),
                                          need[:, :].unsqueeze(1).to_broadcast([P, 16, 16]), ALU.mult))
            step.settle(dve.tensor_reduce(ends[:, :], pref[:, :, :], AX.X, ALU.add))
            step.settle(dve.tensor_tensor(starts[:, :], ends[:, :], need[:, :], ALU.subtract))
            step.mark(dve.tensor_copy(bounds[:, 0, :], starts[:, :]))
            step.mark(dve.tensor_copy(bounds[:, 1, :], ends[:, :]))
            step.settle(dve.tensor_tensor(place[:, :].rearrange(te, e=16), b[1][:, 0:TE].rearrange(te, e=16), offs[:, 0:TILES, :], ALU.add))
            step.settle(dve.tensor_scalar(starts[:, :], starts[:, :], float(P), None, ALU.mult))
            step.settle(dve.tensor_tensor(place[:, :].rearrange(te, e=16), place[:, :].rearrange(te, e=16),
                                          starts[:, :].unsqueeze(1).to_broadcast([P, TILES, 16]), ALU.add))
            for k in range(TOP_K):
                step.settle(dve.tensor_tensor(pick[:, k, :], sel[:, k, :], place[:, :], ALU.mult))
                step.settle(dve.tensor_reduce(slotf[:, k, :], pick[:, k, :].rearrange(te, e=16), AX.X, ALU.add))
            dve.tensor_copy(slots[:, :, :], slotf[:, :, :]).then_inc(s["placed"], 1)

        @block.gpsimd
        def _(pool):
            pool.wait_ge(s["ids_zeroed"], 16)
            pool.wait_ge(s["placed"], 1)
            pool.wait_ge(s["steps"], 1)
            for k in range(TOP_K):
                for t in range(TILES):
                    pool.indirect_dma_start(out=core.slot_ids[:, :], out_offset=bass.IndirectOffsetOnAxis(ap=slots[:, k, t:t + 1], axis=0),
                                            in_=token[:, t:t + 1], in_offset=None).then_inc(s["ids_stored"], 16)


def run_experts(nc, core, ids, bounds, parts, loaded):
    m = core.mem
    W = parts[0]
    rows = m.at("e_rows", AT_XT, [P, D])
    rowsT = m.at("e_rowsT", AT_XT + 4 * KB, [P, KT, P])
    gate = m.at("e_gate", AT_XT + 8 * KB, [P, D_EXPERT])
    hid = m.at("e_hidden", AT_XT + 10 * KB, [P, D_EXPERT])
    hidT = m.at("e_hiddenT", AT_XT + 12 * KB, [P, HT, P])
    y = m.at("e_out", AT_XT + 14 * KB, [P, D])
    index = m.at("e_index", AT_XT + 18 * KB, [P, 1], U32)
    g_bank, u_bank, x_bank, h_bank, y_bank = core.bank[0], core.bank[1], core.bank[2:4], core.bank[4], core.bank[5:7]

    def span(eng, e):
        lo = eng.value_load(bounds[0:1, 0, e:e + 1], min_val=0, max_val=MAX_BLOCKS - 1)
        hi = eng.value_load(bounds[0:1, 1, e:e + 1], min_val=1, max_val=MAX_BLOCKS)
        return eng.Fori(lo, hi)

    with stage(nc, "expert_done", "index_ready", "index_seen", "rows_gathered", "rows_turned", "rowsT_ready0", "rowsT_ready1",
               "gate_ready", "up_ready", "gate_done", "hidden_ready", "hidden_turned", "hiddenT_ready", "out_ready",
               "out_copied0", "out_copied1", "out_stored", "out_free") as (block, s):
        @block.sync
        def _(sp):
            for e in range(1, N_EXPERTS):
                if e >= 2:
                    sp.wait_ge(s["expert_done"], e - 1)
                load_expert(sp, parts, e, loaded[e % 2])

        @block.tensor
        def _(pe):
            def turn_rows(i):
                pe.wait_ge(s["rows_gathered"], (i + 1) * 16)
                for k in range(KT):
                    mm = pe.transpose(x_bank[k // 4][:, (k % 4) * P:(k % 4 + 1) * P], rows[:, k * P:(k + 1) * P], core.c["ident"])
                mm.then_inc(s["rows_turned"], 1)

            pe.sem_inc(s["hidden_turned"])
            turn_rows(0)
            for e in range(N_EXPERTS):
                wg, wu, wd = W[e % 2]
                pe.wait_ge(loaded[e % 2], 48 * (e // 2 + 1))
                with span(pe, e) as i:
                    pe.wait_ge(s["rowsT_ready0"], i + 1)
                    pe.wait_ge(s["rowsT_ready1"], i + 1)
                    pe.wait_ge(s["hidden_ready"], i + 1)
                    for k in range(KT):
                        mm = pe.matmul(g_bank[:, :], rowsT[:, k, :], wg[:, k, :], start=(k == 0), stop=(k == KT - 1))
                    mm.then_inc(s["gate_ready"], 1)
                    for k in range(KT):
                        mm = pe.matmul(u_bank[:, :], rowsT[:, k, :], wu[:, k, :], start=(k == 0), stop=(k == KT - 1))
                    mm.then_inc(s["up_ready"], 1)
                    turn_rows(i + 1)
                    pe.wait_ge(s["hidden_ready"], i + 2)
                    for k in range(HT):
                        mm = pe.transpose(h_bank[:, k * P:(k + 1) * P], hid[:, k * P:(k + 1) * P], core.c["ident"])
                    mm.then_inc(s["hidden_turned"], 1)
                    pe.wait_ge(s["hiddenT_ready"], i + 1)
                    pe.wait_ge(s["out_copied0"], i + 1)
                    pe.wait_ge(s["out_copied1"], i + 1)
                    for half in range(2):
                        for k in range(HT):
                            mm = pe.matmul(y_bank[half][:, :], hidT[:, k, :], wd[:, k, half * BANK:(half + 1) * BANK],
                                           start=(k == 0), stop=(k == HT - 1))
                        mm.then_inc(s["out_ready"], 1)
                pe.drain().then_inc(s["expert_done"], 1)

        @block.scalar
        def _(act):
            def rows_half(i):
                act.wait_ge(s["rows_turned"], i + 1)
                act.activation(rowsT[:, 0:4, :], x_bank[0][:, :].rearrange("p (k q) -> p k q", k=4), ACT.Copy).then_inc(s["rowsT_ready0"], 1)

            act.sem_inc(s["out_copied0"])
            rows_half(0)
            for e in range(N_EXPERTS):
                with span(act, e) as i:
                    act.wait_ge(s["gate_ready"], i + 1)
                    act.wait_ge(s["hidden_ready"], i + 1)
                    act.activation(gate[:, :], g_bank[:, :], ACT.Silu).then_inc(s["gate_done"], 1)
                    rows_half(i + 1)
                    act.wait_ge(s["out_ready"], 2 * i + 1)
                    act.wait_ge(s["out_free"], i + 1)
                    act.activation(y[:, 0:BANK], y_bank[0][:, :], ACT.Copy).then_inc(s["out_copied0"], 1)

        @block.vector
        def _(dve):
            def rows_half(i):
                dve.wait_ge(s["rows_turned"], i + 1)
                dve.tensor_copy(rowsT[:, 4:8, :], x_bank[1][:, :].rearrange("p (k q) -> p k q", k=4)).then_inc(s["rowsT_ready1"], 1)

            dve.sem_inc(s["hidden_ready"])
            dve.sem_inc(s["out_copied1"])
            rows_half(0)
            for e in range(N_EXPERTS):
                with span(dve, e) as i:
                    dve.wait_ge(s["gate_done"], i + 1)
                    dve.wait_ge(s["up_ready"], i + 1)
                    dve.wait_ge(s["hidden_turned"], i + 1)
                    dve.tensor_tensor(hid[:, :], gate[:, :], u_bank[:, :], ALU.mult).then_inc(s["hidden_ready"], 1)
                    rows_half(i + 1)
                    dve.wait_ge(s["hidden_turned"], i + 2)
                    dve.tensor_copy(hidT[:, :, :], h_bank[:, :].rearrange("p (k q) -> p k q", k=HT)).then_inc(s["hiddenT_ready"], 1)
                    dve.wait_ge(s["out_ready"], 2 * i + 2)
                    dve.wait_ge(s["out_free"], i + 1)
                    dve.tensor_copy(y[:, BANK:D], y_bank[1][:, :]).then_inc(s["out_copied1"], 1)

        @block.gpsimd
        def _(pool):
            def gather(i):
                pool.tensor_copy(index[:, :], ids[:, bass.ds(i, 1)]).then_inc(s["index_ready"], 1)
                pool.wait_ge(s["index_ready"], i + 1)
                pool.sem_inc(s["index_seen"])
                pool.indirect_dma_start(out=rows[:, :], out_offset=None, in_=core.token_rows[:, :],
                                        in_offset=bass.IndirectOffsetOnAxis(ap=index[:, :], axis=0)).then_inc(s["rows_gathered"], 16)

            pool.sem_inc(s["out_free"])
            gather(0)
            pool.wait_ge(s["rows_turned"], 1)
            gather(1)
            for e in range(N_EXPERTS):
                with span(pool, e) as i:
                    pool.wait_ge(s["rows_turned"], i + 2)
                    gather(i + 2)
                    pool.wait_ge(s["out_copied0"], i + 2)
                    pool.wait_ge(s["out_copied1"], i + 2)
                    pool.dma_start(core.expert_rows[bass.ds(i * P, P), :], y[:, :]).then_inc(s["out_stored"], 16)
                    pool.wait_ge(s["out_stored"], i * 16 + 16)
                    pool.sem_inc(s["out_free"])
            last = pool.value_load(bounds[0:1, 1, N_EXPERTS - 1:N_EXPERTS], min_val=1, max_val=MAX_BLOCKS)
            pool.wait_ge(s["rows_gathered"], last * 16 + 32)
            pool.wait_ge(s["rows_turned"], last + 1)



ML_HEADS = 4
ML_DH = 192
ML_W = ML_HEADS * ML_DH
HF = ML_DH // 2
ML_TILES = ML_W // HF
CONV_K = 5
DIRS = 2
STREAMS = DIRS * TILES * ML_HEADS
IEXP, CEXP, WEXP, FLOOR = range(4)


def stream(direction, chunk, head):
    return (direction * TILES + chunk) * ML_HEADS + head


def columns_of(vector):
    return vector.rearrange("(n p) -> p n", p=HF)


def ml_layer(nc, core, x, xT):
    m = core.mem
    W = AT_WORK
    slots, lows, highs = ring(core, 192)
    xmT = m.at("ml_xmT", W + 32 * KB, [HF, ML_TILES, SEQ])
    xcT = m.at("ml_xcT", W + 64 * KB, [HF, ML_TILES, SEQ])
    qm = m.at("ml_qm", W + 96 * KB, [P, 2, SEQ])
    gates = m.at("ml_gates", AT_X + 24 * KB, [P, TILES, 16])
    zT = m.at("ml_zT", AT_X, [HF, 4, 2, BANK])
    w = rows_of(core.io["ml_w_in"][0])

    x_parts = Halves(tiles_of(xT), tiles_of(m.at("ml_x_low", AT_XT, [P, KT, SEQ], F32R)), tiles_of(m.at("ml_x_high", W + 64 * KB, [P, KT, SEQ], F32R)))

    def into(c):
        return lambda e, ps, n, half: copy_out(e, xmT[:, 2 * c + n, half * BANK:(half + 1) * BANK], ps)

    def keep_z(c):
        return lambda e, ps, n, half: copy_out(e, zT[:, 2 * c + n, half, :], ps)

    def keep_qm(tile):
        return lambda e, ps, n, half: copy_out(e, qm[:, tile, half * BANK:(half + 1) * BANK], ps, -(HEAD ** -0.5))

    chunks = [(w[:, :, c * 192:(c + 1) * 192], feature_jobs(0, 2, HF, into(c))) for c in range(4)]
    chunks.append((w[:, :, 1536:1680], token_jobs(0, 16, lambda e, ps, t: copy_out(e, gates[:, t, :], ps)) + feature_jobs(16, 1, P, keep_qm(0))))
    chunks.append((w[:, :, 1680:1808], feature_jobs(0, 1, P, keep_qm(1))))
    project(nc, core, chunks, slots, x_parts, lows, highs)
    for c in range(2):
        chunks = [(w[:, :, 768 + (2 * c + i) * 192:960 + (2 * c + i) * 192], feature_jobs(0, 2, HF, keep_z(i))) for i in range(2)]
        project(nc, core, chunks, slots, x_parts, lows, highs)
        store_gate(nc, core, zT, c)
    conv(nc, core, xmT, xcT)

    vals = m.at("ml_v", AT_XT, [P, TILES, ML_HEADS, ML_DH + 1])
    wq = m.at("ml_wqkv", W, [HF, 24, ML_DH])
    hs = m.at("ml_hs", AT_X, [P, TILES, ML_HEADS, ML_DH])
    table = ml_gates(nc, core, gates)
    view = core.io["ml_w_qkv"][0].rearrange("a h (k p) e -> p (a h k) e", p=HF)
    ones_column(nc, core, vals)

    def value_job(h, t):
        return (lambda w, x: [(x[2 * h + k][:, t * P:(t + 1) * P], w[:, (2 * ML_HEADS + h) * 2 + k, :]) for k in range(2)],
                (P, ML_DH), lambda e, ps: copy_out(e, vals[:, t, h, 0:ML_DH], ps))
    project(nc, core, [(view, [value_job(h, t) for h in range(ML_HEADS) for t in range(TILES)])], [wq], tiles_of(xmT))
    for h in range(ML_HEADS):
        qT = m.at("ml_qT", W + 32 * KB, [HF, 2, SEQ])
        kT = m.at("ml_kT", W + 40 * KB, [HF, 2, SEQ])
        keys = m.at("ml_k", AT_XT + 25 * KB, [P, TILES, ML_DH])
        k_scale = ML_DH ** -0.5
        jobs = []
        for a, dst, scale in ((0, qT, None), (1, kT, k_scale)):
            for n in range(2):
                for half in range(2):
                    jobs.append((
                        lambda w, a=a, n=n, half=half: [(wq[:, (a * ML_HEADS + h) * 2 + k, n * HF:(n + 1) * HF],
                                                         xcT[:, 2 * h + k, half * BANK:(half + 1) * BANK]) for k in range(2)],
                        (HF, BANK), lambda e, ps, dst=dst, n=n, half=half, scale=scale:
                        copy_out(e, dst[:, n, half * BANK:(half + 1) * BANK], ps, scale)))
        for t in range(TILES):
            jobs.append((lambda w, t=t: [(xcT[:, 2 * h + k, t * P:(t + 1) * P], wq[:, (ML_HEADS + h) * 2 + k, :]) for k in range(2)],
                         (P, ML_DH), lambda e, ps, t=t: copy_out(e, keys[:, t, :], ps, k_scale)))
        products(nc, core, jobs)
        recurrence(nc, core, h, qT, kT, keys, vals, table, hs)
    head_norm(nc, core, hs, xcT)
    memT = m.at("ml_memT", W + 40 * KB, [P, 2, SEQ])
    memory_attention(nc, core, qm, memT)
    load_rows(nc, core, x, core.token_rows)
    wa = m.at("ml_w_out", W, [HF, ML_TILES, D])
    wb = m.at("ml_w_out_mem", W + 32 * KB, [P, 2, D])
    w_out = core.io["w_out"][1]
    weights = [(w_out[0:ML_W, :].rearrange("(k p) n -> p k n", p=HF), wa[:, :, :]),
               (w_out[ML_W:, :].rearrange("(k p) n -> p k n", p=P), wb[:, :, :])]
    parts = [(xcT[:, k, :], wa[:, k, :]) for k in range(ML_TILES)] + [(memT[:, k, :], wb[:, k, :]) for k in range(2)]
    return parts, weights


def products(nc, core, jobs):
    with stage(nc, "products_ready", "even_emptied", "odd_emptied") as (block, s):
        emptied = [s["even_emptied"], s["odd_emptied"]]

        @block.tensor
        def _(pe):
            for n, (pairs, shape, _) in enumerate(jobs):
                if n >= BANKS:
                    pe.wait_ge(emptied[n % 2], (n - BANKS) // 2 + 1)
                ops = pairs(None)
                for k, (lhsT, rhs) in enumerate(ops):
                    mm = pe.matmul(core.bank[n % BANKS][0:shape[0], 0:shape[1]], lhsT, rhs, start=(k == 0), stop=(k == len(ops) - 1))
                mm.then_inc(s["products_ready"], 1)

        def empty(eng, parity):
            for n in range(parity, len(jobs), 2):
                _, shape, out = jobs[n]
                eng.wait_ge(s["products_ready"], n + 1)
                out(eng, core.bank[n % BANKS][0:shape[0], 0:shape[1]]).then_inc(emptied[parity], 1)

        @block.vector
        def _(dve):
            empty(dve, 0)

        @block.scalar
        def _(act):
            empty(act, 1)


def ones_column(nc, core, vals):
    with stage(nc, "set") as (block, s):
        @block.vector
        def _(dve):
            dve.memset(vals[:, :, :, ML_DH:ML_DH + 1], 1.0).then_inc(s["set"], 1)
            dve.wait_ge(s["set"], 1)


def store_gate(nc, core, zT, c):
    with stage(nc, "silu_done", "stored") as (block, s):
        @block.scalar
        def _(act):
            act.activation(zT[:, :, :, :], zT[:, :, :, :], ACT.Silu).then_inc(s["silu_done"], 1)

        @block.sync
        def _(sp):
            sp.wait_ge(s["silu_done"], 1)
            sp.dma_start(core.gate_rows[:, 4 * c:4 * c + 4, :], zT[:, :, :, :].rearrange("p n a b -> p n (a b)")).then_inc(s["stored"], 16)
            sp.wait_ge(s["stored"], 16)


def conv(nc, core, xmT, xcT):
    m = core.mem
    taps = m.at("conv_w", core.const_end, [HF, ML_TILES, CONV_K])
    bias = m.at("conv_b", core.const_end + 256, [HF, ML_TILES])
    half = CONV_K // 2
    with stage(nc, "loaded", "taps_added", "tile_ready", "tile_done") as (block, s):
        @block.sync
        def _(sp):
            with nc.allow_non_contiguous_dma(reason="a few weights a partition"):
                for j in range(CONV_K):
                    sp.dma_start(taps[:, :, j], columns_of(core.io["ml_conv_w"][0, j])).then_inc(s["loaded"], 16)
                sp.dma_start(bias[:, :], columns_of(core.io["ml_conv_b"][0])).then_inc(s["loaded"], 16)

        @block.vector
        def _(dve):
            step = Steps(dve, s["taps_added"])
            dve.wait_ge(s["loaded"], 16 * (CONV_K + 1))
            for n in range(ML_TILES):
                step.settle(dve.tensor_scalar(xcT[:, n, :], xmT[:, n, :], taps[:, n, half:half + 1], None, ALU.mult))
                others = [j for j in range(CONV_K) if j != half]
                for j in others:
                    d = j - half
                    to = slice(max(0, -d), SEQ - max(0, d))
                    of = slice(max(0, d), SEQ - max(0, -d))
                    ins = dve.scalar_tensor_tensor(out=xcT[:, n, to], in0=xmT[:, n, of], scalar=taps[:, n, j:j + 1],
                                                   in1=xcT[:, n, to], op0=ALU.mult, op1=ALU.add)
                    if j == others[-1]:
                        ins.then_inc(s["tile_ready"], 1)
                    else:
                        step.settle(ins)

        @block.scalar
        def _(act):
            for n in range(ML_TILES):
                act.wait_ge(s["tile_ready"], n + 1)
                act.activation(xcT[:, n, :], xcT[:, n, :], ACT.Silu, bias=bias[:, n:n + 1]).then_inc(s["tile_done"], 1)


class GateTable:

    def __init__(self, a, E, nuT):
        self.a, self.E, self.nuT = a, E, nuT


def ml_gates(nc, core, gates):
    m = core.mem
    o = AT_X + 24 * KB + 512

    def tile(name, cols, rows=P):
        nonlocal o
        t = m.at(name, o, [rows, cols])
        o += (cols * 4 + 31) // 32 * 32
        return t
    S = STREAMS
    H = S // 2
    gb = tile("gate_b", 16)
    ig = tile("i_gate", S)
    fg = tile("f_gate", S)
    ab = tile("f_abs", S)
    lf = tile("log_f", S)
    b = tile("b_sum", S)
    bl = tile("b_last", S)
    a = tile("a", S)
    aT = tile("aT", P, S)
    cm = tile("cummax", P, S)
    peak = tile("peak", 1, S)
    diag = tile("diag", S, S)
    u = tile("u", S)
    ul = tile("u_last", S)
    mc = tile("m_carried", S)
    E = tile("exps", 4 * S)
    nu = tile("neg_u", S)
    nuT = tile("neg_uT", P, S)
    bank = core.bank
    c = core.c

    def col(direction, chunk):
        at = stream(direction, chunk, 0)
        return slice(at, at + ML_HEADS)

    with stage(nc, "loaded", "steps", "exps", "abs_ready", "log_ready", "summands_ready", "sums_ready", "a_ready", "a_turned",
               "cummax_ready", "cummax_turned", "diag_ready", "peaks_ready", "exponents_ready", "exps_ready", "neg_ready", "neg_turned") as (block, s):
        @block.sync
        def _(sp):
            sp.dma_start(gb[:, :], broadcast_rows(core.io["ml_gate_b"][0].rearrange("g h -> (g h)"))).then_inc(s["loaded"], 16)

        @block.tensor
        def _(pe):
            pe.wait_ge(s["summands_ready"], 1)
            pe.matmul(bank[0][:, 0:H], c["upto"], lf[:, 0:H], start=True, stop=True)
            pe.matmul(bank[0][:, H:S], c["from"], lf[:, H:S], start=True, stop=True)
            pe.matmul(bank[0][:, S:2 * S], c["ones"], lf[:, :], start=True, stop=True).then_inc(s["sums_ready"], 1)
            pe.wait_ge(s["a_ready"], 1)
            pe.transpose(bank[1][0:S, 0:P], a[:, :], c["ident"]).then_inc(s["a_turned"], 1)
            pe.wait_ge(s["cummax_ready"], 2)
            pe.transpose(bank[2][:, 0:S], cm[:, :], c["ident"][0:S, 0:S]).then_inc(s["cummax_turned"], 1)
            pe.wait_ge(s["diag_ready"], 1)
            pe.matmul(bank[3][:, 0:S], c["ones"][0:S, :], diag[:, :], start=True, stop=True).then_inc(s["peaks_ready"], 1)
            pe.wait_ge(s["neg_ready"], 1)
            pe.transpose(bank[4][0:S, 0:P], nu[:, :], c["ident"]).then_inc(s["neg_turned"], 1)

        @block.scalar
        def _(act):
            act.wait_ge(s["abs_ready"], 1)
            act.activation(ab[:, :], ab[:, :], ACT.Exp, scale=-1.0).then_inc(s["exps"], 1)
            act.wait_ge(s["exps"], 1)
            act.activation(ab[:, :], ab[:, :], ACT.Ln, bias=c["ones"][:, 0:1]).then_inc(s["log_ready"], 1)
            act.wait_ge(s["exponents_ready"], 1)
            act.activation(E[:, :], E[:, :], ACT.Exp).then_inc(s["exps_ready"], 1)

        @block.vector
        def _(dve):
            step = Steps(dve, s["steps"])
            dve.wait_ge(s["loaded"], 16)
            for t in range(TILES):
                step.mark(dve.tensor_tensor(gates[:, t, :], gates[:, t, :], gb[:, :], ALU.add))
            dve.wait_ge(s["steps"], step.n)
            for d in range(DIRS):
                for gate, dst in ((0, ig), (1, fg)):
                    g0 = (2 * d + gate) * ML_HEADS
                    step.mark(dve.tensor_copy(dst[:, d * H:(d + 1) * H].rearrange("p (t h) -> p t h", h=ML_HEADS), gates[:, :, g0:g0 + ML_HEADS]))
            dve.wait_ge(s["steps"], step.n)
            dve.scalar_tensor_tensor(out=ab[:, :], in0=fg[:, :], scalar=-1.0, in1=fg[:, :], op0=ALU.mult, op1=ALU.max).then_inc(s["abs_ready"], 1)
            step.mark(dve.tensor_scalar(fg[:, :], fg[:, :], 0.0, None, ALU.min))
            dve.wait_ge(s["log_ready"], 1)
            dve.wait_ge(s["steps"], step.n)
            dve.tensor_tensor(lf[:, :], fg[:, :], ab[:, :], ALU.subtract).then_inc(s["summands_ready"], 1)
            dve.wait_ge(s["sums_ready"], 1)
            step.mark(dve.tensor_copy(b[:, :], bank[0][:, 0:S]))
            step.mark(dve.tensor_copy(bl[:, :], bank[0][:, S:2 * S]))
            dve.tensor_tensor(a[:, :], ig[:, :], bank[0][:, 0:S], ALU.subtract).then_inc(s["a_ready"], 1)
            dve.wait_ge(s["a_turned"], 1)
            step.settle(dve.tensor_copy(aT[:, :], bank[1][0:S, 0:P]))
            fwd, bwd = slice(0, H), slice(H, S)
            dve.tensor_tensor_scan(cm[fwd, :], aT[fwd, :], aT[fwd, :], -3.0e38, ALU.max, ALU.max).then_inc(s["cummax_ready"], 1)
            dve.tensor_tensor_scan(cm[bwd, ::-1], aT[bwd, ::-1], aT[bwd, ::-1], -3.0e38, ALU.max, ALU.max).then_inc(s["cummax_ready"], 1)
            step.settle(dve.tensor_reduce(peak[:, :], aT[:, :], AX.X, ALU.max))
            dve.tensor_scalar(diag[:, :], c["ident"][0:S, 0:S], peak[:, 0:1], None, ALU.mult).then_inc(s["diag_ready"], 1)
            step.mark(dve.memset(mc[:, :], 0.0))
            dve.wait_ge(s["peaks_ready"], 1)
            dve.wait_ge(s["steps"], step.n)
            for n in range(TILES):
                for d in range(DIRS):
                    chunk = n if d == 0 else TILES - 1 - n
                    step.mark(dve.tensor_tensor(ul[:, col(d, chunk)], mc[:, col(d, chunk)], bank[3][:, col(d, chunk)], ALU.max))
                dve.wait_ge(s["steps"], step.n)
                if n < TILES - 1:
                    for d in range(DIRS):
                        chunk, after = (n, n + 1) if d == 0 else (TILES - 1 - n, TILES - 2 - n)
                        step.mark(dve.tensor_tensor(mc[:, col(d, after)], ul[:, col(d, chunk)], bl[:, col(d, chunk)], ALU.add))
                    dve.wait_ge(s["steps"], step.n)
            dve.wait_ge(s["cummax_turned"], 1)
            step.settle(dve.tensor_tensor(u[:, :], mc[:, :], bank[2][:, 0:S], ALU.max))
            dve.tensor_scalar(nu[:, :], u[:, :], -1.0, None, ALU.mult).then_inc(s["neg_ready"], 1)
            step.mark(dve.tensor_tensor(E[:, IEXP * S:(IEXP + 1) * S], mc[:, :], u[:, :], ALU.subtract))
            step.mark(dve.tensor_tensor(E[:, CEXP * S:(CEXP + 1) * S], mc[:, :], ul[:, :], ALU.subtract))
            step.mark(dve.tensor_tensor(E[:, WEXP * S:(WEXP + 1) * S], a[:, :], ul[:, :], ALU.subtract))
            dve.wait_ge(s["neg_ready"], 1)
            dve.tensor_tensor(E[:, FLOOR * S:(FLOOR + 1) * S], nu[:, :], b[:, :], ALU.subtract).then_inc(s["exponents_ready"], 1)
            dve.wait_ge(s["neg_turned"], 1)
            step.settle(dve.tensor_copy(nuT[:, :], bank[4][0:S, 0:P]))
    return GateTable(a, E, nuT)


def recurrence(nc, core, h, qT, kT, keys, vals, table, hs):
    m = core.mem
    W = AT_WORK
    U = DIRS * TILES
    DV = ML_DH + 1
    decay = m.at("r_decay", W + 18 * KB, [P, DIRS, TILES, P])
    raw = m.at("r_raw", W + 26 * KB, [P, TILES, P])
    state = m.at("r_state", W + 48 * KB, [HF, DIRS, 2, 2, DV])
    kw = m.at("r_kw", W + 55 * KB, [P, 3, ML_DH])
    carried = m.at("r_carried", W + 58 * KB, [P, 2, DV])
    num = m.at("r_num", W + 60 * KB, [P, 2, DV])
    den = m.at("r_den", W + 62 * KB, [P, U])
    bank, c, E = core.bank, core.c, table.E
    S = STREAMS

    def unit(u):
        n, d = divmod(u, DIRS)
        chunk = n if d == 0 else TILES - 1 - n
        return n, d, chunk, stream(d, chunk, h)

    with stage(nc, "state_zeroed", "spread_ready", "raw_ready", "raw_copied", "masked", "decayed", "probs_ready", "kw_ready", "intra_ready",
               "update_ready", "inter_ready", "carried_ready", "num_ready", "den_steps", "state_ready", "h_ready") as (block, s):
        @block.tensor
        def _(pe):
            for d in range(DIRS):
                for chunk in range(TILES):
                    j = stream(d, chunk, h)
                    mm = pe.matmul(bank[2 * d + chunk // 4][:, (chunk % 4) * P:(chunk % 4 + 1) * P],
                                   c["ident"][0:S, j:j + 1].to_broadcast([S, P]), table.nuT[:, :], start=True, stop=True)
                    if chunk % 4 == 3:
                        mm.then_inc(s["spread_ready"], 1)
            for chunk in range(TILES):
                q = slice(chunk * P, (chunk + 1) * P)
                for k in range(2):
                    mm = pe.matmul(bank[4 + chunk // 4][:, (chunk % 4) * P:(chunk % 4 + 1) * P], kT[:, k, q], qT[:, k, q],
                                   start=(k == 0), stop=(k == 1))
                if chunk % 4 == 3:
                    mm.then_inc(s["raw_ready"], 1)
            pe.wait_ge(s["masked"], 4)
            pe.wait_ge(s["state_zeroed"], 1)
            for u in range(U):
                n, d, chunk, j = unit(u)
                q = slice(chunk * P, (chunk + 1) * P)
                if u < DIRS:
                    pe.wait_ge(s["probs_ready"], u + 1)
                else:
                    pe.wait_ge(s["num_ready"], u - 1)
                pe.matmul(bank[u % 2][:, 0:DV], decay[:, d, chunk, :], vals[:, chunk, h, :], start=True, stop=True).then_inc(s["intra_ready"], 1)
                if n < TILES - 1:
                    pe.wait_ge(s["kw_ready"], u + 1)
                    if u >= 2:
                        pe.wait_ge(s["state_ready"], u - 1)
                    for k in range(2):
                        mm = pe.matmul(bank[6 + u % 2][0:HF, k * 256:k * 256 + DV], kw[:, u % 3, k * HF:(k + 1) * HF], vals[:, chunk, h, :],
                                       start=True, stop=True)
                    mm.then_inc(s["update_ready"], 1)
                if u >= 2:
                    pe.wait_ge(s["state_ready"], u - 1)
                    pe.wait_ge(s["carried_ready"], u - 1)
                for k in range(2):
                    mm = pe.matmul(bank[2 + u % 2][:, 0:DV], qT[:, k, q], state[:, d, n % 2, k, :], start=(k == 0), stop=(k == 1))
                mm.then_inc(s["inter_ready"], 1)

        @block.scalar
        def _(act):
            for g in range(2):
                act.wait_ge(s["raw_ready"], g + 1)
                act.activation(raw[:, 4 * g:4 * g + 4, :].rearrange("p c q -> p (c q)"), bank[4 + g][:, :], ACT.Copy).then_inc(s["raw_copied"], 1)
            for d in range(DIRS):
                for chunk in range(TILES):
                    if chunk % 4 == 0:
                        act.wait_ge(s["masked"], 2 * d + chunk // 4 + 1)
                    j = stream(d, chunk, h)
                    ins = act.activation(decay[:, d, chunk, :], decay[:, d, chunk, :], ACT.Exp, bias=table.a[:, j:j + 1])
                ins.then_inc(s["decayed"], 1)
            for i in range(U + 1):
                if i < U - DIRS:
                    n, d, chunk, j = unit(i)
                    if i >= 3:
                        act.wait_ge(s["update_ready"], i - 2)
                    act.activation(kw[:, i % 3, :], keys[:, chunk, :], ACT.Copy, scale=E[:, WEXP * S + j:WEXP * S + j + 1]).then_inc(s["kw_ready"], 1)
                if i >= 1:
                    u = i - 1
                    n, d, chunk, j = unit(u)
                    act.wait_ge(s["inter_ready"], u + 1)
                    if u >= 2:
                        act.wait_ge(s["num_ready"], u - 1)
                    act.activation(carried[:, u % 2, :], bank[2 + u % 2][:, 0:DV], ACT.Copy,
                                   scale=E[:, IEXP * S + j:IEXP * S + j + 1]).then_inc(s["carried_ready"], 1)

        @block.vector
        def _(dve):
            dve.memset(state[:, :, :, :, :], 0.0).then_inc(s["state_zeroed"], 1)
            for g in range(4):
                dve.wait_ge(s["spread_ready"], g + 1)
                mask = c["neg_future"] if g < 2 else c["neg_past"]
                dve.tensor_tensor(decay[:, g // 2, 4 * (g % 2):4 * (g % 2) + 4, :], bank[g][:, :].rearrange("p (c q) -> p c q", c=4),
                                  mask.unsqueeze(1).to_broadcast([P, 4, P]), ALU.add).then_inc(s["masked"], 1)
            dve.wait_ge(s["raw_copied"], 2)
            for d in range(DIRS):
                dve.wait_ge(s["decayed"], d + 1)
                dve.tensor_tensor(decay[:, d, :, :], decay[:, d, :, :], raw[:, :, :], ALU.mult).then_inc(s["probs_ready"], 1)
            dve.wait_ge(s["state_zeroed"], 1)
            den_step = Steps(dve, s["den_steps"])
            for u in range(U):
                n, d, chunk, j = unit(u)
                if n < TILES - 1:
                    dve.wait_ge(s["update_ready"], u + 1)
                    if u >= 2:
                        dve.wait_ge(s["state_ready"], u - 1)
                        dve.wait_ge(s["inter_ready"], u - 1)
                    dve.scalar_tensor_tensor(out=state[:, d, (n + 1) % 2, :, :], in0=state[:, d, n % 2, :, :],
                                             scalar=E[0:HF, CEXP * S + j:CEXP * S + j + 1],
                                             in1=bank[6 + u % 2][0:HF, :].rearrange("p (k e) -> p k e", k=2)[:, :, 0:DV],
                                             op0=ALU.mult, op1=ALU.add).then_inc(s["state_ready"], 1)
                dve.wait_ge(s["intra_ready"], u + 1)
                dve.wait_ge(s["carried_ready"], u + 1)
                if u >= 2:
                    dve.wait_ge(s["h_ready"], u - 1)
                dve.tensor_tensor(num[:, u % 2, :], carried[:, u % 2, :], bank[u % 2][:, 0:DV], ALU.add).then_inc(s["num_ready"], 1)
                dve.wait_ge(s["num_ready"], u + 1)
                floor = E[:, FLOOR * S + j:FLOOR * S + j + 1]
                raw_den = num[:, u % 2, ML_DH:DV]
                den_step.settle(dve.scalar_tensor_tensor(out=den[:, u:u + 1], in0=raw_den, scalar=-1.0, in1=raw_den, op0=ALU.mult, op1=ALU.max))
                den_step.settle(dve.tensor_scalar(den[:, u:u + 1], den[:, u:u + 1], floor, None, ALU.max))
                den_step.settle(dve.reciprocal(den[:, u:u + 1], den[:, u:u + 1]))
                if n < TILES // 2:
                    ins = dve.tensor_scalar(hs[:, chunk, h, :], num[:, u % 2, 0:ML_DH], den[:, u:u + 1], None, ALU.mult)
                else:
                    first_u = 2 * (TILES - 1 - n) + (1 - d)
                    dve.wait_ge(s["h_ready"], first_u + 1)
                    ins = dve.scalar_tensor_tensor(out=hs[:, chunk, h, :], in0=num[:, u % 2, 0:ML_DH], scalar=den[:, u:u + 1],
                                                   in1=hs[:, chunk, h, :], op0=ALU.mult, op1=ALU.add)
                ins.then_inc(s["h_ready"], 1)


def head_norm(nc, core, hs, xcT):
    m = core.mem
    W = AT_WORK
    R = TILES * ML_HEADS
    stats = m.at("hn_stats", W, [P, R, 6])
    mv = m.at("hn_mv", W + 1 * KB, [P, R, 2])
    rstd = m.at("hn_rstd", W + 2 * KB, [P, R])
    gain = m.at("hn_gain", W + 3 * KB, [HF, ML_TILES])
    skip = m.at("hn_skip", W + 4 * KB, [HF, ML_TILES])
    zT = m.at("hn_z", AT_XT, [HF, ML_TILES, SEQ])
    bank = core.bank
    with stage(nc, "loaded", "gates_loaded", "stats_ready", "variances_ready", "deviations_ready", "inverted", "tile_normed", "turned", "skipped",
               "added", "gated") as (block, s):
        @block.sync
        def _(sp):
            with nc.allow_non_contiguous_dma(reason="a few weights a partition"):
                sp.dma_start(gain[:, :], columns_of(core.io["ml_norm_g"][0])).then_inc(s["loaded"], 16)
                sp.dma_start(skip[:, :], columns_of(core.io["ml_skip"][0])).then_inc(s["loaded"], 16)
            sp.dma_start(zT[:, :, :], core.gate_rows[:, :, :]).then_inc(s["gates_loaded"], 16)

        @block.tensor
        def _(pe):
            pe.wait_ge(s["tile_normed"], TILES)
            for n in range(2 * ML_TILES):
                f, half = divmod(n, 2)
                if n >= BANKS:
                    pe.wait_ge(s["added"], n - BANKS + 1)
                for k in range(4):
                    mm = pe.transpose(bank[n % BANKS][0:HF, k * P:(k + 1) * P],
                                      hs[:, 4 * half + k, f // 2, (f % 2) * HF:(f % 2 + 1) * HF], core.c["ident"])
                mm.then_inc(s["turned"], 1)

        @block.scalar
        def _(act):
            act.wait_ge(s["variances_ready"], R)
            act.activation(rstd[:, :], mv[:, :, 1], ACT.Sqrt, bias=core.c["eps_ln"]).then_inc(s["deviations_ready"], 1)
            act.wait_ge(s["loaded"], 32)
            for f in range(ML_TILES):
                act.activation(xcT[:, f, :], xcT[:, f, :], ACT.Copy, scale=skip[:, f:f + 1]).then_inc(s["skipped"], 1)

        @block.vector
        def _(dve):
            for r in range(R):
                dve.bn_stats(stats[:, r, :], hs[:, r // ML_HEADS, r % ML_HEADS, :]).then_inc(s["stats_ready"], 1)
            for r in range(R):
                dve.wait_ge(s["stats_ready"], r + 1)
                dve.bn_aggr(mv[:, r, :], stats[:, r, :]).then_inc(s["variances_ready"], 1)
            dve.wait_ge(s["deviations_ready"], 1)
            dve.reciprocal(rstd[:, :], rstd[:, :]).then_inc(s["inverted"], 1)
            dve.wait_ge(s["inverted"], 1)
            for t in range(TILES):
                for h in range(ML_HEADS):
                    r = t * ML_HEADS + h
                    ins = dve.tensor_scalar(hs[:, t, h, :], hs[:, t, h, :], mv[:, r, 0:1], rstd[:, r:r + 1], ALU.subtract, ALU.mult)
                ins.then_inc(s["tile_normed"], 1)
            dve.wait_ge(s["loaded"], 32)
            dve.wait_ge(s["gates_loaded"], 16)
            for n in range(2 * ML_TILES):
                f, half = divmod(n, 2)
                q = slice(half * BANK, (half + 1) * BANK)
                dve.wait_ge(s["turned"], n + 1)
                dve.wait_ge(s["skipped"], f + 1)
                dve.scalar_tensor_tensor(out=xcT[:, f, q], in0=bank[n % BANKS][0:HF, :], scalar=gain[:, f:f + 1], in1=xcT[:, f, q],
                                         op0=ALU.mult, op1=ALU.add).then_inc(s["added"], 1)
                if half == 1:
                    dve.wait_ge(s["added"], n + 1)
                    dve.tensor_tensor(xcT[:, f, :], xcT[:, f, :], zT[:, f, :], ALU.mult).then_inc(s["gated"], 1)



RET_W = 256
MLA_HEADS = 8
NOPE = 64
ROPE = 32
MLA_QK = NOPE + ROPE
MLA_W = 512
Q_RANK = 256
KV_RANK = 128
GLA_DK = 32
GLA_KW = 128
GLA_W = 256
GATE_RANK = 16
TAU = 16.0
IN_COLS = 2736
MIX_MLA = RET_W
MIX_GLA = RET_W + MLA_W
TWO_PI_PARTS = (6.25, 0.03125, 0.0019302368, 5.0663948e-06)


def two_pi_parts():
    rest, parts = 2 * np.pi, []
    for bits in (5, 6, 8, 8):
        e = np.floor(np.log2(rest))
        unit = 2.0 ** (e - bits + 1)
        parts.append(float(np.floor(rest / unit) * unit))
        rest -= parts[-1]
    return parts + [float(np.float32(rest))]


def rope_tables(nc, core):
    m = core.mem
    o = AT_WORK
    posi = m.at("pos_i", o, [P, TILES], I32)
    posf = m.at("pos_f", o + 64, [P, TILES])
    ang = m.at("angle", o + 1 * KB, [P, TILES, 32])
    turns = m.at("turns", o + 2 * KB, [P, TILES, 32])
    part = m.at("turn_part", o + 3 * KB, [P, TILES, 32])
    magic = 1.5 * 2.0 ** 23
    pi = float(np.pi)
    with stage(nc, "loaded", "steps", "angles_ready", "tables_ready") as (block, s):
        @block.sync
        def _(sp):
            with nc.allow_non_contiguous_dma(reason="one position a partition"):
                sp.dma_start(posi[:, :], core.io["positions_2"][0].rearrange("(t p) -> p t", p=P)).then_inc(s["loaded"], 16)

        @block.vector
        def _(dve):
            step = Steps(dve, s["steps"])

            def wrap(x):
                for op, edge, turn in ((ALU.is_gt, pi, -2 * pi), (ALU.is_lt, -pi, 2 * pi)):
                    step.settle(dve.tensor_scalar(part[:, :, :], x, edge, turn, op, ALU.mult))
                    step.settle(dve.tensor_tensor(x, x, part[:, :, :], ALU.add))
                step.settle(dve.tensor_scalar(x, x, 3.1415925, -3.1415925, ALU.min, ALU.max))

            dve.wait_ge(s["loaded"], 16)
            step.settle(dve.tensor_copy(posf[:, :], posi[:, :]))
            step.settle(dve.tensor_tensor(ang[:, :, :], posf[:, :].unsqueeze(2).to_broadcast([P, TILES, 32]),
                                          core.c["inv"].unsqueeze(1).to_broadcast([P, TILES, 32]), ALU.mult))
            step.settle(dve.tensor_scalar(turns[:, :, :], ang[:, :, :], 1.0 / (2 * pi), None, ALU.mult))
            step.settle(dve.tensor_scalar(turns[:, :, :], turns[:, :, :], magic, None, ALU.add))
            step.settle(dve.tensor_scalar(turns[:, :, :], turns[:, :, :], -magic, None, ALU.add))
            for c in two_pi_parts():
                step.settle(dve.scalar_tensor_tensor(out=ang[:, :, :], in0=turns[:, :, :], scalar=-c, in1=ang[:, :, :], op0=ALU.mult, op1=ALU.add))
            wrap(ang[:, :, :])
            step.settle(dve.tensor_scalar(turns[:, :, :], ang[:, :, :], pi / 2, None, ALU.add))
            wrap(turns[:, :, :])
            dve.engine_nop().then_inc(s["angles_ready"], 1)

        @block.scalar
        def _(act):
            act.wait_ge(s["angles_ready"], 1)
            act.activation(core.sin[:, :, :], ang[:, :, :], ACT.Sin)
            act.activation(core.cos[:, :, :], turns[:, :, :], ACT.Sin).then_inc(s["tables_ready"], 1)


def rms_of_rows(nc, core, x, rstd, junk):
    with stage(nc, "squared", "root_ready", "inverted") as (block, s):
        @block.scalar
        def _(act):
            for t in range(TILES):
                act.activation(junk[:, t % 2, :], x[:, t, :], ACT.Square, accum_out=rstd[:, t:t + 1]).then_inc(s["squared"], 1)
                act.wait_ge(s["squared"], t + 1)
            act.activation(rstd[:, :], rstd[:, :], ACT.Sqrt, bias=core.c["eps_rms"], scale=1.0 / D).then_inc(s["root_ready"], 1)

        @block.vector
        def _(dve):
            dve.wait_ge(s["root_ready"], 1)
            dve.reciprocal(rstd[:, :], rstd[:, :]).then_inc(s["inverted"], 1)


def modulated_rows(nc, core, x, xT, scale, shift):
    m = core.mem
    rows = m.at("normed_rows", AT_WORK, [P, 2, D])
    rstd = m.at("rstd", core.const_end, [P, TILES])
    rms_of_rows(nc, core, x, rstd, rows)
    with stage(nc, "rows_ready", "turned", "even_emptied", "odd_emptied") as (block, s):
        @block.gpsimd
        def _(pool):
            for t in range(TILES):
                if t >= 2:
                    pool.wait_ge(s["turned"], 2 * t - 2)
                pool.tensor_scalar(rows[:, t % 2, :], x[:, t, :], rstd[:, t:t + 1], None, ALU.mult).then_inc(s["rows_ready"], 1)

        @block.tensor
        def _(pe):
            for n in range(2 * TILES):
                t, k0 = n // 2, (n % 2) * 4
                pe.wait_ge(s["rows_ready"], t + 1)
                if n >= BANKS:
                    pe.wait_ge([s["even_emptied"], s["odd_emptied"]][n % 2], (n - BANKS) // 2 + 1)
                for k in range(4):
                    mm = pe.transpose(core.bank[n % BANKS][:, k * P:(k + 1) * P], rows[:, t % 2, (k0 + k) * P:(k0 + k + 1) * P], core.c["ident"])
                mm.then_inc(s["turned"], 1)

        @block.vector
        def _(dve):
            for n in range(0, 2 * TILES, 2):
                t = n // 2
                dve.wait_ge(s["turned"], n + 1)
                for k in range(4):
                    ins = dve.tensor_scalar(xT[:, k, t * P:(t + 1) * P], core.bank[n % BANKS][:, k * P:(k + 1) * P],
                                            scale[:, k:k + 1], shift[:, k:k + 1], ALU.mult, ALU.add)
                ins.then_inc(s["even_emptied"], 1)

        @block.scalar
        def _(act):
            for n in range(1, 2 * TILES, 2):
                t = n // 2
                act.wait_ge(s["turned"], n + 1)
                for k in range(4):
                    ins = act.activation(xT[:, 4 + k, t * P:(t + 1) * P], core.bank[n % BANKS][:, k * P:(k + 1) * P], ACT.Identity,
                                         scale=scale[:, 4 + k:5 + k], bias=shift[:, 4 + k:5 + k])
                ins.then_inc(s["odd_emptied"], 1)


def rotate(step, x1, x2, cos, sin, tmp):
    dve = step.eng
    for dst, a, b in ((tmp[0], x1, cos), (tmp[1], x2, sin), (tmp[2], x2, cos), (tmp[3], x1, sin)):
        step.mark(dve.tensor_tensor(dst, a, b, ALU.mult))
    dve.wait_ge(step.sem, step.n)
    step.mark(dve.tensor_tensor(x1, tmp[0], tmp[1], ALU.subtract))
    step.mark(dve.tensor_tensor(x2, tmp[2], tmp[3], ALU.add))
    dve.wait_ge(step.sem, step.n)


def gated_heads(nc, core, y, z, heads, gain=None):
    m = core.mem
    W = heads * HEAD
    sq = m.at("gh_sq", AT_WORK + 24 * KB, [P, TILES, W])
    ms = m.at("gh_ms", core.const_end, [P, TILES * heads])
    gr = m.at("gh_gain", core.const_end + 256, [P, HEAD])
    hd = "p (r d) -> p r d"
    with stage(nc, "loaded", "squares_ready", "sums_ready", "roots_ready", "steps", "silu_done") as (block, s):
        if gain is not None:
            @block.sync
            def _(sp):
                sp.dma_start(gr[:, :], broadcast_rows(gain)).then_inc(s["loaded"], 16)

        @block.scalar
        def _(act):
            for t in range(TILES):
                act.activation(sq[:, t, :], y[:, t, :], ACT.Square).then_inc(s["squares_ready"], 1)
            act.activation(z, z, ACT.Silu).then_inc(s["silu_done"], 1)
            act.wait_ge(s["sums_ready"], 1)
            act.activation(ms[:, :], ms[:, :], ACT.Sqrt, bias=core.c["eps_rms"], scale=1.0 / HEAD).then_inc(s["roots_ready"], 1)

        @block.vector
        def _(dve):
            step = Steps(dve, s["steps"])
            dve.wait_ge(s["squares_ready"], TILES)
            dve.tensor_reduce(ms[:, :], sq[:, :, :].rearrange("p t (h d) -> p (t h) d", h=heads), AX.X, ALU.add).then_inc(s["sums_ready"], 1)
            dve.wait_ge(s["silu_done"], 1)
            step.settle(dve.tensor_tensor(y, y, z, ALU.mult))
            if gain is not None:
                dve.wait_ge(s["loaded"], 16)
                step.settle(dve.tensor_tensor(y.rearrange("p t (h d) -> p t h d", h=heads), y.rearrange("p t (h d) -> p t h d", h=heads),
                                              gr[:, :].unsqueeze(1).unsqueeze(1).to_broadcast([P, TILES, heads, HEAD]), ALU.mult))
            dve.wait_ge(s["roots_ready"], 1)
            step.settle(dve.reciprocal(ms[:, :], ms[:, :]))
            step.mark(dve.tensor_tensor(y.rearrange("p t (h d) -> p t h d", h=heads), y.rearrange("p t (h d) -> p t h d", h=heads),
                                        ms[:, :].rearrange("p (t h) -> p t h", h=heads).unsqueeze(3).to_broadcast([P, TILES, heads, HEAD]), ALU.mult))


def retention(nc, core, qk, v, out):
    m = core.mem
    W = AT_WORK
    qkT = m.at("ret_qkT", W, [P, 4, SEQ])
    tmp = [m.at(f"ret_rot{i}", W + 8 * i * KB, [P, TILES, 8, 32]) for i in range(4)]
    with stage(nc, "steps") as (block, s):
        @block.vector
        def _(dve):
            step = Steps(dve, s["steps"])
            heads = qk[:, :, :].rearrange("p t (h d) -> p t h d", h=8)
            shape = [P, TILES, 8, 32]
            rotate(step, heads[:, :, :, 0:32], heads[:, :, :, 32:64], core.cos[:, :, :].unsqueeze(2).to_broadcast(shape),
                   core.sin[:, :, :].unsqueeze(2).to_broadcast(shape), [t[:, :, :, :] for t in tmp])
    transpose_rows(nc, core, qk, qkT, cols=4)
    kw = m.at("ret_kw", W + 16 * KB, [P, 2, RET_W])
    probs = m.at("ret_probs", W + 18 * KB, [P, 2, 2, 2, P])
    state = m.at("ret_state", W + 22 * KB, [P, 2, 2, HEAD])
    scaled = m.at("ret_scaled", W + 23 * KB, [P, 2, HEAD])
    carried = m.at("ret_carried", W + 24 * KB, [P, 2, 2, 2, HEAD])
    bank, c = core.bank, core.c
    k_of = qk[:, :, RET_W:2 * RET_W]
    with stage(nc, "state_ready", "kw_ready", "raw_ready", "probs_ready", "intra_ready", "update_ready", "inter_ready", "scaled_ready",
               "carried_ready", "out_ready") as (block, s):
        @block.tensor
        def _(pe):
            pe.wait_ge(s["state_ready"], 1)
            for u in range(TILES):
                q = slice(u * P, (u + 1) * P)
                if u >= 1:
                    pe.wait_ge(s["probs_ready"], 2 * u)
                for h in range(RET_HEADS):
                    p0 = (h % 2) * HEAD
                    mm = pe.matmul(bank[h % 2][:, (h // 2) * P:(h // 2 + 1) * P], qkT[p0:p0 + HEAD, 2 + h // 2, q],
                                   qkT[p0:p0 + HEAD, h // 2, q], start=True, stop=True)
                mm.then_inc(s["raw_ready"], 1)
                if u < TILES - 1:
                    pe.wait_ge(s["kw_ready"], u + 1)
                    if u >= 1:
                        pe.wait_ge(s["state_ready"], u + 1)
                    for h in range(RET_HEADS):
                        p0 = (h % 2) * HEAD
                        mm = pe.matmul(bank[2][p0:p0 + HEAD, (h // 2) * HEAD:(h // 2 + 1) * HEAD], kw[:, u % 2, h * HEAD:(h + 1) * HEAD],
                                       v[:, u, h * HEAD:(h + 1) * HEAD], start=True, stop=True)
                    mm.then_inc(s["update_ready"], 1)
                pe.wait_ge(s["state_ready"], u + 1)
                if u >= 1:
                    pe.wait_ge(s["carried_ready"], u)
                for h in range(RET_HEADS):
                    p0 = (h % 2) * HEAD
                    mm = pe.matmul(bank[4 + h % 2][:, (h // 2) * HEAD:(h // 2 + 1) * HEAD], qkT[p0:p0 + HEAD, h // 2, q],
                                   state[p0:p0 + HEAD, u % 2, h // 2, :], start=True, stop=True)
                mm.then_inc(s["inter_ready"], 1)
                pe.wait_ge(s["probs_ready"], 2 * u + 2)
                if u >= 2:
                    pe.wait_ge(s["out_ready"], u - 1)
                for h in range(RET_HEADS):
                    mm = pe.matmul(bank[6 + u % 2][:, h * HEAD:(h + 1) * HEAD], probs[:, u % 2, h % 2, h // 2, :],
                                   v[:, u, h * HEAD:(h + 1) * HEAD], start=True, stop=True)
                mm.then_inc(s["intra_ready"], 1)

        @block.gpsimd
        def _(pool):
            for u in range(TILES - 1):
                if u >= 2:
                    pool.wait_ge(s["update_ready"], u - 1)
                pool.tensor_tensor(kw[:, u % 2, :].rearrange("p (h d) -> p h d", h=RET_HEADS),
                                   k_of[:, u, :].rearrange("p (h d) -> p h d", h=RET_HEADS),
                                   c["ret_k"].unsqueeze(2).to_broadcast([P, RET_HEADS, HEAD]), ALU.mult).then_inc(s["kw_ready"], 1)

        @block.scalar
        def _(act):
            for u in range(TILES):
                act.wait_ge(s["inter_ready"], u + 1)
                if u >= 2:
                    act.wait_ge(s["out_ready"], u - 1)
                for h in range(RET_HEADS):
                    ins = act.activation(carried[:, u % 2, h // 2, h % 2, :], bank[4 + h % 2][:, (h // 2) * HEAD:(h // 2 + 1) * HEAD], ACT.Copy,
                                         scale=c["ret_q"][:, h:h + 1])
                ins.then_inc(s["carried_ready"], 1)

        @block.vector
        def _(dve):
            dve.memset(state[:, 0, :, :], 0.0).then_inc(s["state_ready"], 1)
            for u in range(TILES):
                dve.wait_ge(s["raw_ready"], u + 1)
                if u >= 2:
                    dve.wait_ge(s["intra_ready"], u - 1)
                for side in range(2):
                    for pair in range(2):
                        ins = dve.tensor_tensor(probs[:, u % 2, side, pair, :], bank[side][:, pair * P:(pair + 1) * P], c[f"decay{2 * pair + side}"], ALU.mult)
                    ins.then_inc(s["probs_ready"], 1)
                if u < TILES - 1:
                    dve.wait_ge(s["state_ready"], u + 1)
                    dve.tensor_tensor(scaled[:, :, :], state[:, u % 2, :, :], c["ret_carry"].unsqueeze(2).to_broadcast([P, 2, HEAD]), ALU.mult).then_inc(s["scaled_ready"], 1)
                    dve.wait_ge(s["scaled_ready"], u + 1)
                    dve.wait_ge(s["update_ready"], u + 1)
                    if u >= 1:
                        dve.wait_ge(s["inter_ready"], u)
                    dve.tensor_tensor(state[:, (u + 1) % 2, :, :], scaled[:, :, :], bank[2][:, 0:2 * HEAD].rearrange("p (a d) -> p a d", a=2),
                                      ALU.add).then_inc(s["state_ready"], 1)
                dve.wait_ge(s["intra_ready"], u + 1)
                dve.wait_ge(s["carried_ready"], u + 1)
                dve.tensor_tensor(out[:, u, :], bank[6 + u % 2][:, 0:RET_W], carried[:, u % 2].rearrange("p a b d -> p (a b d)"),
                                  ALU.add).then_inc(s["out_ready"], 1)


def gated_linear(nc, core, l, g1, g2, out):
    m = core.mem
    W = AT_WORK
    bank, c = core.bank, core.c
    lowT = m.at("gla_lowT", W, [GATE_RANK, SEQ])
    w2 = m.at("gla_w2", W + 4 * KB, [GATE_RANK, GLA_KW])
    b2 = m.at("gla_b2", W + 5 * KB, [P, GLA_KW])
    la = m.at("gla_log_a", W + 6 * KB, [P, TILES, GLA_KW])
    ab = m.at("gla_abs", W + 10 * KB, [P, TILES, GLA_KW])
    last = m.at("gla_last", core.const_end + 1 * KB, [P, 2 * TILES])
    e_pos = m.at("gla_e_pos", W + 14 * KB, [P, TILES, GLA_KW])
    e_neg = m.at("gla_e_neg", W + 18 * KB, [P, TILES, GLA_KW])
    e_end = m.at("gla_e_end", W + 22 * KB, [P, TILES, GLA_KW])
    prods = m.at("gla_prods", W + 32 * KB, [P, TILES, 4, GLA_KW])
    prodT = m.at("gla_prodT", W + 48 * KB, [P, 4, SEQ])
    q, k, v = g1[:, :, 0:GLA_KW], g1[:, :, GLA_KW:2 * GLA_KW], g1[:, :, 2 * GLA_KW:]
    k_scale = GLA_DK ** -0.5
    with stage(nc, "loaded", "low_turned", "low_copied", "gate_products", "steps", "abs_ready", "exps", "logs_ready", "log_a_ready",
               "sums_ready", "exp_ready", "end_ready") as (block, s):
        @block.sync
        def _(sp):
            sp.dma_start(w2[:, :], core.io["gla_w_g2_2"][l]).then_inc(s["loaded"], 16)
            sp.dma_start(b2[:, :], broadcast_rows(core.io["gla_b_g2_2"][l])).then_inc(s["loaded"], 16)

        @block.tensor
        def _(pe):
            for t in range(TILES):
                mm = pe.transpose(bank[t // 4][0:GATE_RANK, (t % 4) * P:(t % 4 + 1) * P], g2[:, t, 0:GATE_RANK], c["ident"])
            mm.then_inc(s["low_turned"], 1)
            pe.wait_ge(s["loaded"], 32)
            pe.wait_ge(s["low_copied"], 1)
            for t in range(TILES):
                mm = pe.matmul(bank[2 + t // 4][:, (t % 4) * P:(t % 4 + 1) * P], lowT[:, t * P:(t + 1) * P], w2[:, :], start=True, stop=True)
            mm.then_inc(s["gate_products"], 1)
            pe.wait_ge(s["log_a_ready"], 1)
            for half in range(2):
                rows = la[:, 4 * half:4 * half + 4, :].rearrange("p t f -> p (t f)")
                pe.matmul(bank[4 + half][:, :], c["chunk_upto"], rows, start=True, stop=True)
                pe.matmul(bank[6 + half][:, :], c["chunk_all"], rows, start=True, stop=True)
            for t in range(TILES):
                mm = pe.matmul(bank[0][:, 2 * t:2 * t + 2], la[:, t, :], c["chunk_of"], start=True, stop=True)
            mm.then_inc(s["sums_ready"], 1)

        @block.scalar
        def _(act):
            act.wait_ge(s["low_turned"], 1)
            act.activation(lowT[:, :].rearrange("p (b n) -> p b n", b=2), core.psum[0:GATE_RANK, 0:2, :], ACT.Copy).then_inc(s["low_copied"], 1)
            act.wait_ge(s["abs_ready"], 1)
            act.activation(ab[:, :, :], ab[:, :, :], ACT.Exp, scale=-1.0).then_inc(s["exps"], 1)
            act.wait_ge(s["exps"], 1)
            act.activation(ab[:, :, :], ab[:, :, :], ACT.Ln, bias=c["ones"][:, 0:1]).then_inc(s["logs_ready"], 1)
            act.wait_ge(s["sums_ready"], 1)
            for half in range(2):
                cols = slice(4 * half, 4 * half + 4)
                act.activation(e_pos[:, cols, :].rearrange("p t f -> p (t f)"), bank[4 + half][:, :], ACT.Exp)
                act.activation(e_neg[:, cols, :].rearrange("p t f -> p (t f)"), bank[4 + half][:, :], ACT.Exp, scale=-1.0)
            act.activation(last[:, :], bank[0][:, 0:2 * TILES], ACT.Exp).then_inc(s["exp_ready"], 1)
            act.wait_ge(s["end_ready"], 1)
            act.activation(e_end[:, :, :], e_end[:, :, :], ACT.Exp).then_inc(s["exp_ready"], 1)

        @block.vector
        def _(dve):
            step = Steps(dve, s["steps"])
            dve.wait_ge(s["loaded"], 32)
            dve.wait_ge(s["gate_products"], 1)
            flat = "p t f -> p (t f)"
            for half in range(2):
                step.mark(dve.tensor_tensor(la[:, 4 * half:4 * half + 4, :], bank[2 + half][:, :].rearrange("p (t f) -> p t f", t=4),
                                            b2[:, :].unsqueeze(1).to_broadcast([P, 4, GLA_KW]), ALU.add))
            dve.wait_ge(s["steps"], step.n)
            dve.scalar_tensor_tensor(out=ab[:, :, :], in0=la[:, :, :], scalar=-1.0, in1=la[:, :, :], op0=ALU.mult, op1=ALU.max).then_inc(s["abs_ready"], 1)
            dve.wait_ge(s["logs_ready"], 1)
            step.settle(dve.scalar_tensor_tensor(out=la[:, :, :], in0=la[:, :, :], scalar=0.0, in1=ab[:, :, :], op0=ALU.min, op1=ALU.subtract))
            dve.tensor_scalar(la[:, :, :], la[:, :, :], 1.0 / TAU, None, ALU.mult).then_inc(s["log_a_ready"], 1)
            dve.wait_ge(s["sums_ready"], 1)
            step.mark(dve.tensor_copy(e_end[:, :, :].rearrange("p (b t) f -> p b (t f)", b=2), core.psum[:, 6:8, :]))
            dve.wait_ge(s["steps"], step.n)
            dve.wait_ge(s["exp_ready"], 1)
            dve.tensor_tensor(e_end[:, :, :].rearrange("p (b t) f -> p b (t f)", b=2), e_end[:, :, :].rearrange("p (b t) f -> p b (t f)", b=2),
                              core.psum[:, 4:6, :], ALU.subtract).then_inc(s["end_ready"], 1)
            step.settle(dve.tensor_scalar(k, k, k_scale, None, ALU.mult))
            dve.wait_ge(s["exp_ready"], 1)
            for n, (a, b) in enumerate(((q, e_pos), (q, e_neg), (k, e_neg), (k, e_pos))):
                step.mark(dve.tensor_tensor(prods[:, :, n, :], a, b[:, :, :], ALU.mult))
            dve.wait_ge(s["steps"], step.n)
            dve.wait_ge(s["exp_ready"], 2)
            step.mark(dve.tensor_tensor(k, k, e_end[:, :, :], ALU.mult))
    transpose_rows(nc, core, prods[:, :, :, :].rearrange("p t n f -> p t (n f)"), prodT, cols=4)

    states = m.at("gla_states", W, [P, 2 * TILES, GLA_W])
    attn = m.at("gla_attn", W + 16 * KB, [P, GLA_HEADS, 2, P])
    NC = 2 * TILES
    mask = [c["gla_past"].bitcast(U32), c["gla_future"].bitcast(U32)]
    GROUPS = TILES // 2
    with stage(nc, "zeroed", "scores_ready", "past_set", "attn_ready", "intra_ready", "update_ready", "state_ready", "inter_ready", "inter_copied", "out_ready") as (block, s):
        @block.tensor
        def _(pe):
            for n in range(NC - 1):
                r0 = (n % 2) * CHUNK_2
                if n >= 4:
                    pe.wait_ge(s["state_ready"], n - 3)
                pe.matmul(bank[4 + n % 4][:, 0:GLA_W], k[r0:r0 + CHUNK_2, n // 2, :], v[r0:r0 + CHUNK_2, n // 2, :],
                          start=True, stop=True).then_inc(s["update_ready"], 1)
            pe.wait_ge(s["zeroed"], 1)
            pe.wait_ge(s["state_ready"], NC - 1)
            for g in range(GROUPS):
                if g >= 1:
                    pe.wait_ge(s["attn_ready"], g)
                for i in range(2):
                    t = 2 * g + i
                    cols = slice(t * P, (t + 1) * P)
                    for side, (a, b) in enumerate(((2, 0), (3, 1))):
                        for h in range(GLA_HEADS):
                            p0 = h * GLA_DK
                            mm = pe.matmul(bank[h][:, (2 * i + side) * P:(2 * i + side + 1) * P], prodT[p0:p0 + GLA_DK, a, cols],
                                           prodT[p0:p0 + GLA_DK, b, cols], start=True, stop=True)
                mm.then_inc(s["scores_ready"], 1)
                if g >= 2:
                    pe.wait_ge(s["inter_copied"], g - 1)
                for i in range(2):
                    for half in range(2):
                        n = 2 * (2 * g + i) + half
                        r0 = half * CHUNK_2
                        mm = pe.matmul(bank[4 + g % 2][r0:r0 + CHUNK_2, i * GLA_W:(i + 1) * GLA_W],
                                       prodT[:, 0, n * CHUNK_2:(n + 1) * CHUNK_2], states[:, n, :], start=True, stop=True)
                mm.then_inc(s["inter_ready"], 1)
                pe.wait_ge(s["attn_ready"], g + 1)
                if g >= 2:
                    pe.wait_ge(s["out_ready"], g - 1)
                for i in range(2):
                    for h in range(GLA_HEADS):
                        mm = pe.matmul(bank[6 + g % 2][:, i * GLA_W + h * HEAD:i * GLA_W + (h + 1) * HEAD], attn[:, h, i, :],
                                       v[:, 2 * g + i, h * HEAD:(h + 1) * HEAD], start=True, stop=True)
                mm.then_inc(s["intra_ready"], 1)

        @block.scalar
        def _(act):
            for g in range(GROUPS):
                act.wait_ge(s["inter_ready"], g + 1)
                act.activation(out[:, 2 * g:2 * g + 2, :], bank[4 + g % 2][:, :].rearrange("p (i e) -> p i e", i=2), ACT.Copy).then_inc(s["inter_copied"], 1)

        @block.vector
        def _(dve):
            dve.memset(states[:, :, :], 0.0)
            dve.memset(attn[:, :, :, :], 0.0).then_inc(s["zeroed"], 1)
            dve.wait_ge(s["zeroed"], 1)
            for n in range(NC - 1):
                dve.wait_ge(s["update_ready"], n + 1)
                if n >= 1:
                    dve.wait_ge(s["state_ready"], n)
                for h in range(GLA_HEADS):
                    rows = slice(h * GLA_DK, (h + 1) * GLA_DK)
                    cols = slice(h * HEAD, (h + 1) * HEAD)
                    ins = dve.scalar_tensor_tensor(out=states[rows, n + 1, cols], in0=states[rows, n, cols], scalar=last[rows, n:n + 1],
                                                   in1=bank[4 + n % 4][rows, cols], op0=ALU.mult, op1=ALU.add)
                ins.then_inc(s["state_ready"], 1)
            for g in range(GROUPS):
                dve.wait_ge(s["scores_ready"], g + 1)
                if g >= 1:
                    dve.wait_ge(s["intra_ready"], g)
                for side, done in enumerate((s["past_set"], s["attn_ready"])):
                    for h in range(GLA_HEADS):
                        raw = bank[h][:, :].rearrange("p (i s q) -> p i s q", i=2, s=2)
                        ins = dve.copy_predicated(attn[:, h, :, :], mask[side].unsqueeze(1).to_broadcast([P, 2, P]), raw[:, :, side, :])
                    ins.then_inc(done, 1)
                    dve.wait_ge(done, g + 1)
                dve.wait_ge(s["intra_ready"], g + 1)
                dve.wait_ge(s["inter_copied"], g + 1)
                dve.tensor_tensor(out[:, 2 * g:2 * g + 2, :], out[:, 2 * g:2 * g + 2, :], bank[6 + g % 2][:, :].rearrange("p (i e) -> p i e", i=2),
                                  ALU.add).then_inc(s["out_ready"], 1)


def latent_attention(nc, core, l, m1, mz, out):
    m = core.mem
    W = AT_WORK
    c = core.c
    qlT = m.at("mla_qlT", W + 24 * KB, [P, 2, SEQ])
    kvT = m.at("mla_kvT", W + 109 * KB, [P, SEQ])
    w_ukv = m.at("mla_w_ukv", W + 113 * KB, [P, MLA_HEADS * P])
    w_uq = m.at("mla_w_uq", W + 56 * KB, [P, 2, MLA_HEADS * MLA_QK])
    Q = m.at("mla_q", W, [P, TILES, MLA_HEADS * MLA_QK])
    V = m.at("mla_v", W + 93 * KB, [P, TILES, MLA_W])
    sq = m.at("mla_sq", W, [P, TILES, Q_RANK + KV_RANK])
    ms = m.at("mla_ms", core.const_end, [P, 2, TILES])
    qn = m.at("mla_qn", core.const_end + 128, [P, 2])
    kn = m.at("mla_kn", core.const_end + 192, [P, 1])
    lat = Q_RANK + KV_RANK
    rot = [m.at(f"mla_krot{i}", W + 20 * KB + 512 * i, [P, TILES, 16]) for i in range(4)]
    cos16, sin16 = core.cos[:, :, 0:32:2], core.sin[:, :, 0:32:2]
    with stage(nc, "loaded", "squares_ready", "sums_ready", "roots_ready", "steps") as (block, s):
        @block.sync
        def _(sp):
            sp.dma_start(w_uq[:, :, :], rows_of(core.io["w_uq_2"][l])).then_inc(s["loaded"], 16)
            sp.dma_start(w_ukv[:, :], core.io["w_ukv_2"][l]).then_inc(s["loaded"], 16)
            with nc.allow_non_contiguous_dma(reason="a few weights a partition"):
                sp.dma_start(qn[:, :], core.io["mla_q_norm_2"][l].rearrange("(k p) -> p k", p=P)).then_inc(s["loaded"], 16)
                sp.dma_start(kn[:, :], core.io["mla_kv_norm_2"][l].rearrange("(p a) -> p a", a=1)).then_inc(s["loaded"], 16)
            sp.wait_ge(s["loaded"], 64)

        @block.scalar
        def _(act):
            act.activation(sq[:, :, :], m1[:, :, 0:lat], ACT.Square).then_inc(s["squares_ready"], 1)
            act.wait_ge(s["sums_ready"], 1)
            for n, rank in enumerate((Q_RANK, KV_RANK)):
                ins = act.activation(ms[:, n, :], ms[:, n, :], ACT.Sqrt, bias=c["eps_rms"], scale=1.0 / rank)
            ins.then_inc(s["roots_ready"], 1)

        @block.vector
        def _(dve):
            step = Steps(dve, s["steps"])
            rotate(step, m1[:, :, lat:lat + 16], m1[:, :, lat + 16:lat + 32], cos16, sin16, [t[:, :, :] for t in rot])
            dve.wait_ge(s["squares_ready"], 1)
            dve.tensor_reduce(ms[:, 0, :], sq[:, :, 0:Q_RANK], AX.X, ALU.add)
            dve.tensor_reduce(ms[:, 1, :], sq[:, :, Q_RANK:lat], AX.X, ALU.add).then_inc(s["sums_ready"], 1)
            dve.wait_ge(s["roots_ready"], 1)
            step.settle(dve.reciprocal(ms[:, :, :], ms[:, :, :]))
            step.mark(dve.tensor_tensor(m1[:, :, 0:Q_RANK], m1[:, :, 0:Q_RANK], ms[:, 0, :].unsqueeze(2).to_broadcast([P, TILES, Q_RANK]), ALU.mult))
            step.mark(dve.tensor_tensor(m1[:, :, Q_RANK:lat], m1[:, :, Q_RANK:lat], ms[:, 1, :].unsqueeze(2).to_broadcast([P, TILES, KV_RANK]), ALU.mult))
    kT = m.at("mla_kT", W + 32 * KB, [MLA_QK, MLA_HEADS, SEQ])
    with stage(nc, "turned", "emptied_even", "emptied_odd") as (block, s):
        emptied = [s["emptied_even"], s["emptied_odd"]]

        @block.tensor
        def _(pe):
            for n in range(6):
                k, half = divmod(n, 2)
                for i in range(4):
                    mm = pe.transpose(core.bank[n][:, i * P:(i + 1) * P], m1[:, 4 * half + i, k * P:(k + 1) * P], c["ident"])
                mm.then_inc(s["turned"], 1)

        def empty(eng, parity):
            for n in range(parity, 6, 2):
                k, half = divmod(n, 2)
                q = slice(half * BANK, (half + 1) * BANK)
                eng.wait_ge(s["turned"], n + 1)
                dst, w = (qlT[:, k, q], qn[:, k:k + 1]) if k < 2 else (kvT[:, q], kn[:, 0:1])
                copy_out(eng, dst, core.bank[n], w).then_inc(emptied[parity], 1)

        @block.vector
        def _(dve):
            empty(dve, 0)

        @block.scalar
        def _(act):
            empty(act, 1)
    jobs = []
    for t in range(TILES):
        for half in range(2):
            cols = slice(half * 384, (half + 1) * 384)
            jobs.append((lambda w, t=t, cols=cols: [(qlT[:, k, t * P:(t + 1) * P], w_uq[:, k, cols]) for k in range(2)], (P, 384),
                         lambda e, ps, t=t, cols=cols: copy_out(e, Q[:, t, cols], ps)))
        jobs.append((lambda w, t=t: [(kvT[:, t * P:(t + 1) * P], w_ukv[:, :].rearrange("p (h e) -> p h e", h=MLA_HEADS)[:, :, NOPE:])], (P, MLA_W),
                     lambda e, ps, t=t: copy_out(e, V[:, t, :], ps)))
    products(nc, core, jobs)
    jobs = []
    for h in range(MLA_HEADS):
        for half in range(2):
            q = slice(half * BANK, (half + 1) * BANK)
            jobs.append((lambda w, h=h, q=q: [(w_ukv[:, h * P:h * P + NOPE], kvT[:, q])], (NOPE, BANK),
                         lambda e, ps, h=h, q=q: copy_out(e, kT[0:NOPE, h, q], ps)))
    products(nc, core, jobs)
    rot = [m.at(f"mla_qrot{i}", W + 24 * KB + 4 * i * KB, [P, TILES, MLA_HEADS, 16]) for i in range(2)]
    rot += [m.at(f"mla_qrot{i}", W + 109 * KB + 4 * i * KB, [P, TILES, MLA_HEADS, 16]) for i in range(2)]
    with stage(nc, "steps", "turned", "copied") as (block, s):
        @block.tensor
        def _(pe):
            for t in range(TILES):
                mm = pe.transpose(core.bank[t // 4][0:ROPE, (t % 4) * P:(t % 4 + 1) * P], m1[:, t, lat:lat + ROPE], c["ident"])
            mm.then_inc(s["turned"], 1)

        @block.scalar
        def _(act):
            act.wait_ge(s["turned"], 1)
            for h in range(MLA_HEADS):
                act.activation(kT[NOPE:MLA_QK, h, :].rearrange("p (b n) -> p b n", b=2), core.psum[0:ROPE, 0:2, :], ACT.Copy).then_inc(s["copied"], 1)

        @block.vector
        def _(dve):
            step = Steps(dve, s["steps"])
            heads = Q[:, :, :].rearrange("p t (h d) -> p t h d", h=MLA_HEADS)
            shape = [P, TILES, MLA_HEADS, 16]
            rotate(step, heads[:, :, :, NOPE:NOPE + 16], heads[:, :, :, NOPE + 16:MLA_QK], cos16.unsqueeze(2).to_broadcast(shape),
                   sin16.unsqueeze(2).to_broadcast(shape), [t[:, :, :, :] for t in rot])

    probs = m.at("mla_probs", W + 24 * KB, [P, 2, SEQ])
    probsT = m.at("mla_probsT", W + 64 * KB, [P, 2, SEQ])
    qT = m.at("mla_qT", W + 72 * KB, [MLA_QK, 2, P])
    low = m.at("mla_low", W + 73 * KB, [P, 64])
    sums = m.at("mla_sums", W + 73 * KB + 256, [P, 64])
    inv = m.at("mla_inv", W + 73 * KB + 512, [P, 64])
    units = [(h, i) for h in range(MLA_HEADS) for i in range(TILES)]
    U = len(units)
    s_pair = [core.psum[:, 0:2, :], core.psum[:, 2:4, :]]
    t_bank, o_bank, q_bank = [core.bank[4], core.bank[5]], core.bank[6], core.bank[7]

    def spans(i):
        n = (i + 1) * P
        return [(b, min(BANK, n - b * BANK)) for b in range((n + BANK - 1) // BANK)]
    with stage(nc, "q_turned", "q_copied", "scores_ready", "lows_ready", "probs_ready", "turned", "copied0", "copied1", "values_ready",
               "inverted", "out_ready", "silu_done", "gated") as (block, s):
        @block.tensor
        def _(pe):
            def turn_q(u):
                h, i = units[u]
                if u >= 1:
                    pe.wait_ge(s["q_copied"], u)
                pe.transpose(q_bank[0:MLA_QK, 0:P], Q[:, i, h * MLA_QK:(h + 1) * MLA_QK], c["ident"]).then_inc(s["q_turned"], 1)

            def scores(u):
                h, i = units[u]
                pe.wait_ge(s["q_copied"], u + 1)
                if u >= 2:
                    pe.wait_ge(s["probs_ready"], u - 1)
                for b, n in spans(i):
                    n -= P if b == i // 4 else 0
                    if n:
                        pe.matmul(s_pair[u % 2][:, b, 0:n], qT[:, u % 2, :], kT[:, h, b * BANK:b * BANK + n], start=True, stop=True)
                last = s_pair[u % 2][:, i // 4, (i % 4) * P:(i % 4 + 1) * P]
                pe.matmul(last, qT[:, u % 2, :], kT[:, h, i * P:(i + 1) * P], start=True, stop=False)
                pe.matmul(last, c["early"][0:1, :], c["late_big"][0:1, :], start=False, stop=True).then_inc(s["scores_ready"], 1)

            def turn(u):
                h, i = units[u]
                pe.wait_ge(s["probs_ready"], u + 1)
                if u >= 1:
                    pe.wait_ge(s["copied0"], u)
                    pe.wait_ge(s["copied1"], u)
                for k in range(i + 1):
                    mm = pe.transpose(t_bank[k // 4][:, (k % 4) * P:(k % 4 + 1) * P], probs[:, u % 2, k * P:(k + 1) * P], c["ident"])
                mm.then_inc(s["turned"], 1)

            def values(u):
                h, i = units[u]
                pe.wait_ge(s["copied0"], u + 1)
                pe.wait_ge(s["copied1"], u + 1)
                if u >= 1:
                    pe.wait_ge(s["out_ready"], u)
                for k in range(i + 1):
                    mm = pe.matmul(o_bank[:, (u % 2) * HEAD:(u % 2 + 1) * HEAD], probsT[:, u % 2, k * P:(k + 1) * P], V[:, k, h * HEAD:(h + 1) * HEAD],
                                   start=(k == 0), stop=(k == i))
                mm.then_inc(s["values_ready"], 1)

            turn_q(0)
            for i in range(U + 2):
                if i + 1 < U:
                    turn_q(i + 1)
                if i < U:
                    scores(i)
                if 1 <= i < U + 1:
                    turn(i - 1)
                if 2 <= i:
                    values(i - 2)

        @block.vector
        def _(dve):
            def copy_q(u):
                dve.wait_ge(s["q_turned"], u + 1)
                if u >= 2:
                    dve.wait_ge(s["scores_ready"], u - 1)
                dve.tensor_scalar(qT[:, u % 2, :], q_bank[0:MLA_QK, 0:P], -(MLA_QK ** -0.5), None, ALU.mult).then_inc(s["q_copied"], 1)

            copy_q(0)
            for n in range(U + 2):
                if n + 1 < U:
                    copy_q(n + 1)
                if n < U:
                    h, i = units[n]
                    dve.wait_ge(s["scores_ready"], n + 1)
                    cols = (i + 1) * P
                    flat = s_pair[n % 2].rearrange("p b n -> p (b n)")[:, 0:cols]
                    dve.tensor_reduce(low[:, n:n + 1], flat, AX.X, ALU.min).then_inc(s["lows_ready"], 1)
                if 1 <= n < U + 1:
                    u = n - 1
                    h, i = units[u]
                    dve.wait_ge(s["turned"], u + 1)
                    if u >= 2:
                        dve.wait_ge(s["values_ready"], u - 1)
                    w = min(i + 1, 4) * P
                    dve.tensor_copy(probsT[:, u % 2, 0:w], t_bank[0][:, 0:w]).then_inc(s["copied0"], 1)
                if n >= 2:
                    u = n - 2
                    h, i = units[u]
                    dve.reciprocal(inv[:, u:u + 1], sums[:, u:u + 1]).then_inc(s["inverted"], 1)
                    dve.wait_ge(s["inverted"], u + 1)
                    dve.wait_ge(s["values_ready"], u + 1)
                    dve.tensor_scalar(out[:, i, h * HEAD:(h + 1) * HEAD], o_bank[:, (u % 2) * HEAD:(u % 2 + 1) * HEAD], inv[:, u:u + 1], None,
                                      ALU.mult).then_inc(s["out_ready"], 1)
            dve.wait_ge(s["out_ready"], U)
            dve.wait_ge(s["silu_done"], 1)
            dve.tensor_tensor(out, out, mz[:, :, :], ALU.mult).then_inc(s["gated"], 1)

        @block.scalar
        def _(act):
            act.activation(mz[:, :, :], mz[:, :, :], ACT.Silu).then_inc(s["silu_done"], 1)
            for n in range(U + 1):
                if n < U:
                    h, i = units[n]
                    cols = (i + 1) * P
                    act.wait_ge(s["lows_ready"], n + 1)
                    if n >= 2:
                        act.wait_ge(s["turned"], n - 1)
                    act.activation(probs[:, n % 2, 0:cols], s_pair[n % 2].rearrange("p b n -> p (b n)")[:, 0:cols], ACT.Exp,
                                   bias=low[:, n:n + 1], scale=-1.0, accum_out=sums[:, n:n + 1]).then_inc(s["probs_ready"], 1)
                if n >= 1:
                    u = n - 1
                    h, i = units[u]
                    act.wait_ge(s["turned"], u + 1)
                    if i < 4:
                        act.sem_inc(s["copied1"], 1)
                        continue
                    if u >= 2:
                        act.wait_ge(s["values_ready"], u - 1)
                    act.activation(probsT[:, u % 2, BANK:(i + 1) * P], t_bank[1][:, 0:(i - 3) * P], ACT.Copy).then_inc(s["copied1"], 1)


def second_layer(nc, core, l, x):
    m = core.mem
    W = AT_WORK
    xT = m.at("s_xT", AT_XT, [P, KT, SEQ])
    mod = core.modulations[l]
    modulated_rows(nc, core, x, xT, mod.scale, mod.shift)
    slots, lows, highs = ring(core, 2 * P)
    x_parts = Halves(tiles_of(xT), tiles_of(m.at("s_x_low", AT_XT, [P, KT, SEQ], F32R)), tiles_of(m.at("s_x_high", AT_X, [P, KT, SEQ], F32R)))
    widths = [512, 512, 416, 512, 512, 272]
    at, tiles, chunks = W + 32 * KB, [], []
    w = rows_of(core.io["w_in_2"][l])
    c0 = 0
    for n, width in enumerate(widths):
        tile = m.at(f"proj{n}", at, [P, TILES, width])
        at += TILES * width * 4
        tiles.append(tile)
        for part in range(2):
            cols = slice(part * width // 2, (part + 1) * width // 2)
            chunks.append((w[:, :, c0 + cols.start:c0 + cols.stop],
                           token_jobs(0, width // 2, lambda e, ps, t, tile=tile, cols=cols: copy_out(e, tile[:, t, cols], ps))))
        c0 += width
    project(nc, core, chunks, slots, x_parts, lows, highs)
    x = m.at("s_x", AT_X, [P, TILES, D])
    r_qk, r_vz, m1, mz, g1, g2 = tiles
    mix = m.at("s_mix", AT_XT, [P, TILES, D])
    retention(nc, core, r_qk, r_vz[:, :, 0:RET_W], mix[:, :, 0:RET_W])
    gated_heads(nc, core, mix[:, :, 0:RET_W], r_vz[:, :, RET_W:], RET_HEADS)
    gated_linear(nc, core, l, g1, g2, mix[:, :, MIX_GLA:])
    gated_heads(nc, core, mix[:, :, MIX_GLA:], g2[:, :, GATE_RANK:], GLA_HEADS, core.io["gla_norm_2"][l])
    latent_attention(nc, core, l, m1, mz, mix[:, :, MIX_MLA:MIX_GLA])
    mixT = m.at("s_mixT", W, [P, KT, SEQ])
    w_out = m.at("s_w_out", W + 32 * KB, [P, KT, D])
    transpose_rows(nc, core, mix, mixT)
    gated_residual(nc, core, x, mixT, w_out, core.io["w_out_2"][l], mod.gate, spill=l < DEPTH - 1)
    return x


def gated_residual(nc, core, x, mixT, w_out, w_dram, gate, spill):
    m = core.mem
    W = AT_WORK
    tmp = m.at("gr_tmp", W + 64 * KB, [P, 2, BANK])
    mix_low = m.at("gr_mix_low", W, [P, KT, SEQ], F32R)
    mix_high = m.at("gr_mix_high", AT_XT, [P, KT, SEQ], F32R)
    w_low = m.at("gr_w_low", W + 32 * KB, [P, KT, D], F32R)
    w_high = m.at("gr_w_high", W + 72 * KB, [P, KT, D], F32R)
    rows = core.token_rows.rearrange("(t p) d -> p t d", p=P)
    HALF = KT // 2
    with stage(nc, "weights_loaded0", "weights_loaded1", "x_loaded", "high_ready", "low_ready", "products_ready", "gated", "added", "stored") as (block, s):
        @block.sync
        def _(sp):
            for g in range(2):
                sp.dma_start(w_out[:, g * HALF:(g + 1) * HALF, :], rows_of(w_dram)[:, g * HALF:(g + 1) * HALF, :]).then_inc(s[f"weights_loaded{g}"], 16)
            sp.dma_start(x[:, :, :], rows).then_inc(s["x_loaded"], 16)
            if spill:
                for t in range(TILES):
                    sp.wait_ge(s["added"], 2 * t + 2)
                    sp.dma_start(rows[:, t, :], x[:, t, :]).then_inc(s["stored"], 16)
                sp.wait_ge(s["stored"], 16 * TILES)

        @block.tensor
        def _(pe):
            for n in range(2 * TILES):
                t, half = divmod(n, 2)
                rows_, cols = slice(t * P, (t + 1) * P), slice(half * BANK, (half + 1) * BANK)
                if n >= BANKS:
                    pe.wait_ge(s["gated"], n - BANKS + 1)
                for k in range(KT):
                    if n == 0:
                        pe.wait_ge(s["high_ready"], 2 * k + 2)
                    pe.matmul(core.bank[n % BANKS], mix_high[:, k, rows_], w_high[:, k, cols], start=(k == 0), stop=False)
                for k in range(KT):
                    if n == 0:
                        pe.wait_ge(s["low_ready"], 2 * k + 2)
                    pe.matmul(core.bank[n % BANKS], mix_high[:, k, rows_], w_low[:, k, cols], start=False, stop=False)
                    mm = pe.matmul(core.bank[n % BANKS], mix_low[:, k, rows_], w_high[:, k, cols], start=False, stop=(k == KT - 1))
                mm.then_inc(s["products_ready"], 1)

        @block.scalar
        def _(act):
            for k in range(KT):
                act.activation(mix_high[:, k, :], mixT[:, k, :], ACT.Copy).then_inc(s["high_ready"], 1)
                if k % HALF == 0:
                    act.wait_ge(s[f"weights_loaded{k // HALF}"], 16)
                act.activation(w_high[:, k, :], w_out[:, k, :], ACT.Copy).then_inc(s["high_ready"], 1)

        @block.vector
        def _(dve):
            for k in range(KT):
                dve.wait_ge(s["high_ready"], 2 * k + 1)
                leave_low(dve, mix_low[:, k, :], mixT[:, k, :], mix_high[:, k, :]).then_inc(s["low_ready"], 1)
                dve.wait_ge(s[f"weights_loaded{k // HALF}"], 16)
                dve.wait_ge(s["high_ready"], 2 * k + 2)
                leave_low(dve, w_low[:, k, :], w_out[:, k, :], w_high[:, k, :]).then_inc(s["low_ready"], 1)
            dve.wait_ge(s["x_loaded"], 16)
            for n in range(2 * TILES):
                t, half = divmod(n, 2)
                cols = slice(half * BANK, (half + 1) * BANK)
                dve.wait_ge(s["products_ready"], n + 1)
                if n >= 2:
                    dve.wait_ge(s["added"], n - 1)
                dve.tensor_tensor(tmp[:, n % 2, :], core.bank[n % BANKS], gate[:, cols], ALU.mult).then_inc(s["gated"], 1)
                dve.wait_ge(s["gated"], n + 1)
                dve.tensor_tensor(x[:, t, cols], x[:, t, cols], tmp[:, n % 2, :], ALU.add).then_inc(s["added"], 1)


def final_rows(nc, core, x, out, gain, s_out):
    m = core.mem
    junk = m.at("final_junk", AT_WORK, [P, 2, D])
    rstd = m.at("final_rstd", core.const_end, [P, TILES])
    g_rows = m.at("final_gain", AT_WORK + 8 * KB, [P, D])
    rms_of_rows(nc, core, x, rstd, junk)
    view = out.rearrange("(t p) d -> p t d", p=P)
    with stage(nc, "loaded", "scaled") as (block, s):
        @block.sync
        def _(sp):
            sp.dma_start(g_rows[:, :], broadcast_rows(gain)).then_inc(s["loaded"], 16)
            for t in range(TILES):
                sp.wait_ge(s["scaled"], t + 1)
                sp.dma_start(view[:, t, :], x[:, t, :]).then_inc(s_out, 16)
            sp.wait_ge(s_out, 16 * TILES)

        @block.vector
        def _(dve):
            dve.wait_ge(s["loaded"], 16)
            for t in range(TILES):
                dve.scalar_tensor_tensor(out=x[:, t, :], in0=x[:, t, :], scalar=rstd[:, t:t + 1], in1=g_rows[:, :],
                                         op0=ALU.mult, op1=ALU.mult).then_inc(s["scaled"], 1)


def first_block(nc, core):
    m = core.mem
    io = core.io
    memory_rows(nc, core)
    mixT = na_layer(nc, core)
    x = m.at("x", AT_X, [P, TILES, D])
    xT = m.at("xT", AT_XT, [P, KT, SEQ])
    load_rows(nc, core, x, io["x"][0])
    w_out = m.at("w_out", AT_WORK, [P, KT, D])
    residual_norm(nc, core, x, xT, io["ln_g"][0, 0], io["ln_b"][0, 0], parts=[(mixT[:, k, :], w_out[:, k, :]) for k in range(KT)],
                  weights=[(rows_of(io["w_out"][0]), w_out[:, :, :])], spill=core.token_rows)
    experts = moe(nc, core, 0, x, xT)
    residual_norm(nc, core, x, xT, io["ln_g"][0, 1], io["ln_b"][0, 1], experts=experts, spill=core.token_rows,
                  beside=core.modulations[0])
    parts, weights = ml_layer(nc, core, x, xT)
    residual_norm(nc, core, x, xT, io["ln_g"][1, 0], io["ln_b"][1, 0], parts=parts, weights=weights, spill=core.token_rows)
    experts = moe(nc, core, 1, x, xT)
    residual_norm(nc, core, x, None, io["ln_g"][1, 1], io["ln_b"][1, 1], experts=experts, spill=core.token_rows,
                  beside=core.modulations[1])
    return x


def build_program(nc, io, out):
    core = make_core(nc, io)
    out_stored = nc.alloc_semaphore("out_stored")
    rope_tables(nc, core)
    core.modulations = [Modulation(core, l) for l in range(DEPTH)]
    x = first_block(nc, core)
    for l in range(DEPTH):
        x = second_layer(nc, core, l, x)
    final_rows(nc, core, x, out, io["final_norm_2"], out_stored)


def kernel(**inputs):
    import concourse.bacc as bacc
    from concourse.bass_utils import run_bass_kernel_spmd

    nc = bacc.Bacc("TRN2", target_bir_lowering=False, num_devices=1)
    arrays, io = {}, {}
    inputs["na_rpb"] = inputs["na_rpb"][..., ::-1]
    for name, a in {**inputs, "consts": const_table()}.items():
        a = np.ascontiguousarray(a)
        arrays[f"in_{name}"] = a
        io[name] = nc.dram_tensor(f"in_{name}", a.shape, mybir.dt.from_np(a.dtype), kind="ExternalInput").ap()
    out = nc.dram_tensor("out_rows", (1, SEQ, D), F32, kind="ExternalOutput").ap()
    build_program(nc, io, out[0])
    r = run_bass_kernel_spmd(nc, [arrays], core_ids=[0])
    return r.results[0]["out_rows"]
```
